# Optimizing a Trainium2 kernel written in Bass

```python
import math
import jax, jax.numpy as jnp
from jax import lax
import numpy as np

D_MODEL = 1024
BATCH = 1
SEQ = 256
DEPTH = 1

HEAD_DIM = 64
SWA_Q_HEADS = 8
SWA_KV_HEADS = 2
SWA_WINDOW = 128
MOBA_Q_HEADS = 8
MOBA_KV_HEADS = 2
MOBA_BLOCK = 256
MOBA_TOPK = 3
MOBA_Q_CHUNK = 32
N_HEADS = SWA_Q_HEADS + MOBA_Q_HEADS
REL_BUCKETS = 32
REL_MAX_DIST = 128
N_GROUPS = 4
EXPERTS_PER_GROUP = 8
N_EXPERTS = N_GROUPS * EXPERTS_PER_GROUP
EXPERT_TOPK = 2
D_EXPERT = 512
DISPATCH_BLOCK = 256
PLE_DIM = 256
EPS = 1e-6
NEG = -1e30

SWA_Q_W = SWA_Q_HEADS * HEAD_DIM
SWA_KV_W = SWA_KV_HEADS * HEAD_DIM
MOBA_Q_W = MOBA_Q_HEADS * HEAD_DIM
MOBA_KV_W = MOBA_KV_HEADS * HEAD_DIM
MIX_W = SWA_Q_W + MOBA_Q_W
IN_W = SWA_Q_W + 2 * SWA_KV_W + MOBA_Q_W + 2 * MOBA_KV_W
SPLITS = [SWA_Q_W, SWA_Q_W + SWA_KV_W, SWA_Q_W + 2 * SWA_KV_W,
          SWA_Q_W + 2 * SWA_KV_W + MOBA_Q_W, SWA_Q_W + 2 * SWA_KV_W + MOBA_Q_W + MOBA_KV_W]

kernel_name = 'hymba_swa_sink_moba_hiermoe_ple'

def rms_norm(x, g):
    xf = x.astype(jnp.float32)
    y = xf * lax.rsqrt(jnp.mean(xf * xf, axis=-1, keepdims=True) + EPS)
    return (y * g.astype(jnp.float32)).astype(x.dtype)

def rel_bucket(dist):
    n = jnp.maximum(dist, 0)
    exact = REL_BUCKETS // 2
    nf = jnp.maximum(n, 1).astype(jnp.float32)
    large = exact + (jnp.log(nf / exact) / math.log(REL_MAX_DIST / exact)
                     * (REL_BUCKETS - exact)).astype(jnp.int32)
    return jnp.where(n < exact, n, jnp.minimum(large, REL_BUCKETS - 1))

def swa_attention(q, k, v, sinks, rel_tbl):
    B, S = q.shape[0], q.shape[1]
    W = SWA_WINDOW
    NB = S // W
    G = SWA_KV_HEADS
    R = SWA_Q_HEADS // G
    qb = q.reshape(B, NB, W, G, R, HEAD_DIM)
    pad = ((0, 0), (W, 0), (0, 0), (0, 0))
    kp = jnp.pad(k, pad).reshape(B, NB + 1, W, G, HEAD_DIM)
    vp = jnp.pad(v, pad).reshape(B, NB + 1, W, G, HEAD_DIM)
    kband = jnp.concatenate([kp[:, :-1], kp[:, 1:]], axis=2)
    vband = jnp.concatenate([vp[:, :-1], vp[:, 1:]], axis=2)
    qi = jnp.arange(W)[:, None]
    kj = jnp.arange(2 * W)[None, :]
    dist = qi + W - kj
    band = (dist >= 0) & (dist < W)
    key_pos = (jnp.arange(NB)[:, None, None] - 1) * W + kj[None]
    mask = band[None] & (key_pos >= 0)
    bias = rel_tbl.astype(jnp.float32)[rel_bucket(dist)]
    bias = bias.transpose(2, 0, 1).reshape(G, R, W, 2 * W)
    s = jnp.einsum('bnqgrd,bnkgd->bngrqk', qb, kband).astype(jnp.float32) * HEAD_DIM ** -0.5 + bias
    s = jnp.where(mask[None, :, None, None], s, NEG)
    sink = sinks.astype(jnp.float32).reshape(G, R)[None, None, :, :, None, None]
    m = jnp.maximum(jnp.max(s, axis=-1, keepdims=True), sink)
    e = jnp.exp(s - m)
    prob = e / (jnp.sum(e, axis=-1, keepdims=True) + jnp.exp(sink - m))
    o = jnp.einsum('bngrqk,bnkgd->bnqgrd', prob.astype(v.dtype), vband)
    return o.reshape(B, S, SWA_Q_W)

def moba_attention(q, k, v, rel_tbl):
    B, S = q.shape[0], q.shape[1]
    G = MOBA_KV_HEADS
    R = MOBA_Q_HEADS // G
    BS = MOBA_BLOCK
    C = MOBA_Q_CHUNK
    NBK = -(-S // BS)
    S_pad = NBK * BS
    K = min(MOBA_TOPK, NBK)
    NC = S // C
    scale = HEAD_DIM ** -0.5
    qh = q.reshape(B, S, G, R, HEAD_DIM).transpose(0, 2, 3, 1, 4)
    pad = ((0, 0), (0, S_pad - S), (0, 0), (0, 0))
    kT = jnp.pad(k, pad).transpose(0, 2, 1, 3)
    vT = jnp.pad(v, pad).transpose(0, 2, 1, 3)
    kblk = kT.reshape(B, G, NBK, BS, HEAD_DIM)
    vblk = vT.reshape(B, G, NBK, BS, HEAD_DIM)
    kmean = jnp.mean(kblk.astype(jnp.float32), axis=3)
    gate = jnp.einsum('bgrsd,bgnd->bgrsn', qh.astype(jnp.float32), kmean)
    fully_past = jnp.arange(NBK)[None, :] < (jnp.arange(S) // BS)[:, None]
    gate = jnp.where(fully_past, gate, NEG)
    _, sel = lax.top_k(gate, K)
    tbl = rel_tbl.astype(jnp.float32).T.reshape(G, R, REL_BUCKETS)
    bi = jnp.arange(B)[:, None, None, None, None]
    gi = jnp.arange(G)[None, :, None, None, None]
    gi6 = jnp.arange(G)[None, :, None, None, None, None]
    ri6 = jnp.arange(R)[None, None, :, None, None, None]

    def chunk(args):
        c, qc, selc = args
        q0 = c * C
        own_blk = q0 // BS
        qpos = q0 + jnp.arange(C)
        kg = kblk[bi, gi, selc]
        vg = vblk[bi, gi, selc]
        s_past = jnp.einsum('bgrcd,bgrcksd->bgrcks', qc, kg).astype(jnp.float32) * scale
        kpos = selc[..., None] * BS + jnp.arange(BS)
        s_past = s_past + tbl[gi6, ri6, rel_bucket(qpos[:, None, None] - kpos)]
        valid = jnp.arange(K) < jnp.minimum(K, own_blk)
        s_past = jnp.where(valid[:, None], s_past, NEG)
        own_start = own_blk * BS
        k_own = lax.dynamic_slice_in_dim(kT, own_start, BS, axis=2)
        v_own = lax.dynamic_slice_in_dim(vT, own_start, BS, axis=2)
        s_own = jnp.einsum('bgrcd,bgsd->bgrcs', qc, k_own).astype(jnp.float32) * scale
        d_own = qpos[:, None] - (own_start + jnp.arange(BS))[None, :]
        s_own = s_own + tbl[:, :, rel_bucket(d_own)]
        s_own = jnp.where(d_own >= 0, s_own, NEG)
        s_all = jnp.concatenate([s_past.reshape(B, G, R, C, K * BS), s_own], axis=-1)
        prob = jax.nn.softmax(s_all, axis=-1).astype(v.dtype)
        p_past = prob[..., :K * BS].reshape(B, G, R, C, K, BS)
        return (jnp.einsum('bgrcks,bgrcksd->bgrcd', p_past, vg)
                + jnp.einsum('bgrcs,bgsd->bgrcd', prob[..., K * BS:], v_own))

    q_chunks = qh.reshape(B, G, R, NC, C, HEAD_DIM).transpose(3, 0, 1, 2, 4, 5)
    sel_chunks = sel.reshape(B, G, R, NC, C, K).transpose(3, 0, 1, 2, 4, 5)
    o = lax.map(chunk, (jnp.arange(NC), q_chunks, sel_chunks))
    return o.transpose(1, 0, 4, 2, 3, 5).reshape(B, S, MOBA_Q_W)

def hier_moe(h, w_rg, b_rg, w_re, b_re, w_g, w_u, w_d):
    T, D = h.shape
    A = T * EXPERT_TOPK
    M = DISPATCH_BLOCK
    NBLK = -(-A // M) + N_EXPERTS
    P = NBLK * M
    glog = (h @ w_rg).astype(jnp.float32) + b_rg.astype(jnp.float32)
    gprob = jax.nn.softmax(glog, axis=-1)
    gsel = jnp.argmax(glog, axis=-1)
    gw = jnp.take_along_axis(gprob, gsel[:, None], axis=1)
    elog = ((h @ w_re).astype(jnp.float32) + b_re.astype(jnp.float32)).reshape(T, N_GROUPS, EXPERTS_PER_GROUP)
    elog = jnp.take_along_axis(elog, gsel[:, None, None], axis=1)[:, 0]
    top_v, top_i = lax.top_k(elog, EXPERT_TOPK)
    w = gw * jax.nn.softmax(top_v, axis=-1)
    eid = (gsel[:, None] * EXPERTS_PER_GROUP + top_i).reshape(A)
    wflat = w.reshape(A)
    counts = jnp.bincount(eid, length=N_EXPERTS)
    start = jnp.cumsum(counts) - counts
    padded = (counts + M - 1) // M * M
    pad_end = jnp.cumsum(padded)
    pad_start = pad_end - padded
    order = jnp.argsort(eid)
    es = eid[order]
    tok = order // EXPERT_TOPK
    dest = pad_start[es] + (jnp.arange(A) - start[es])
    x_buf = jnp.zeros((P, D), h.dtype).at[dest].set(h[tok])
    block_expert = jnp.minimum(jnp.searchsorted(pad_end, jnp.arange(NBLK) * M, side='right'), N_EXPERTS - 1)

    def run_block(args):
        xb, e = args
        return (jax.nn.silu(xb @ w_g[e]) * (xb @ w_u[e])) @ w_d[e]

    out_buf = lax.map(run_block, (x_buf.reshape(NBLK, M, D), block_expert)).reshape(P, D)
    return jnp.zeros((T, D), h.dtype).at[tok].add(out_buf[dest] * wflat[order][:, None].astype(h.dtype))

def setup_inputs(seed: int = 0) -> dict:
    key = jax.random.key(seed)
    ks = jax.random.split(key, 26)
    f = jnp.float32
    def nrm(k, shape, scale):
        return jax.random.normal(k, shape, f) * scale
    def gain(k, shape):
        return 1.0 + 0.05 * jax.random.normal(k, shape, f)
    L = DEPTH
    return {
        'x': nrm(ks[0], (BATCH, SEQ, D_MODEL), 1.0),
        'p': nrm(ks[1], (DEPTH, BATCH, SEQ, PLE_DIM), 1.0),
        'rel_bias': nrm(ks[2], (REL_BUCKETS, N_HEADS), 0.2),
        'attn_norm': gain(ks[3], (L, D_MODEL)),
        'w_in': nrm(ks[4], (L, D_MODEL, IN_W), D_MODEL ** -0.5),
        'swa_q_norm': gain(ks[5], (L, HEAD_DIM)),
        'swa_k_norm': gain(ks[6], (L, HEAD_DIM)),
        'swa_sinks': nrm(ks[7], (L, SWA_Q_HEADS), 0.5),
        'moba_q_norm': gain(ks[8], (L, HEAD_DIM)),
        'moba_k_norm': gain(ks[9], (L, HEAD_DIM)),
        'swa_out_norm': gain(ks[10], (L, SWA_Q_W)),
        'moba_out_norm': gain(ks[11], (L, MOBA_Q_W)),
        'w_out': nrm(ks[12], (L, MIX_W, D_MODEL), MIX_W ** -0.5),
        'ffn_norm': gain(ks[13], (L, D_MODEL)),
        'w_router_group': nrm(ks[14], (L, D_MODEL, N_GROUPS), D_MODEL ** -0.5),
        'b_router_group': nrm(ks[15], (L, N_GROUPS), 0.01),
        'w_router_expert': nrm(ks[16], (L, D_MODEL, N_EXPERTS), D_MODEL ** -0.5),
        'b_router_expert': nrm(ks[17], (L, N_EXPERTS), 0.01),
        'w_exp_gate': nrm(ks[18], (L, N_EXPERTS, D_MODEL, D_EXPERT), D_MODEL ** -0.5),
        'w_exp_up': nrm(ks[19], (L, N_EXPERTS, D_MODEL, D_EXPERT), D_MODEL ** -0.5),
        'w_exp_down': nrm(ks[20], (L, N_EXPERTS, D_EXPERT, D_MODEL), D_EXPERT ** -0.5),
        'ple_norm': gain(ks[21], (L, D_MODEL)),
        'w_ple_gate': nrm(ks[22], (L, D_MODEL, D_MODEL), D_MODEL ** -0.5),
        'w_ple_proj': nrm(ks[23], (L, PLE_DIM, D_MODEL), PLE_DIM ** -0.5),
        'ple_out_norm': gain(ks[24], (L, D_MODEL)),
    }

def reference(x, p, rel_bias, attn_norm, w_in, swa_q_norm, swa_k_norm, swa_sinks,
              moba_q_norm, moba_k_norm, swa_out_norm, moba_out_norm, w_out, ffn_norm,
              w_router_group, b_router_group, w_router_expert, b_router_expert,
              w_exp_gate, w_exp_up, w_exp_down, ple_norm, w_ple_gate, w_ple_proj, ple_out_norm):
    B, S, D = x.shape
    swa_tbl = rel_bias[:, :SWA_Q_HEADS]
    moba_tbl = rel_bias[:, SWA_Q_HEADS:]
    for i in range(DEPTH):
        h = rms_norm(x, attn_norm[i])
        qa, ka, va, qb, kb, vb = jnp.split(h @ w_in[i], SPLITS, axis=-1)
        qa = rms_norm(qa.reshape(B, S, SWA_Q_HEADS, HEAD_DIM), swa_q_norm[i])
        ka = rms_norm(ka.reshape(B, S, SWA_KV_HEADS, HEAD_DIM), swa_k_norm[i])
        va = va.reshape(B, S, SWA_KV_HEADS, HEAD_DIM)
        qb = rms_norm(qb.reshape(B, S, MOBA_Q_HEADS, HEAD_DIM), moba_q_norm[i])
        kb = rms_norm(kb.reshape(B, S, MOBA_KV_HEADS, HEAD_DIM), moba_k_norm[i])
        vb = vb.reshape(B, S, MOBA_KV_HEADS, HEAD_DIM)
        o_a = swa_attention(qa, ka, va, swa_sinks[i], swa_tbl)
        o_b = moba_attention(qb, kb, vb, moba_tbl)
        mix = jnp.concatenate([rms_norm(o_a, swa_out_norm[i]), rms_norm(o_b, moba_out_norm[i])], axis=-1)
        x = x + mix @ w_out[i]
        hf = rms_norm(x, ffn_norm[i]).reshape(B * S, D)
        x = x + hier_moe(hf, w_router_group[i], b_router_group[i], w_router_expert[i], b_router_expert[i],
                         w_exp_gate[i], w_exp_up[i], w_exp_down[i]).reshape(B, S, D)
        gate = jax.nn.sigmoid(rms_norm(x, ple_norm[i]) @ w_ple_gate[i])
        x = x + gate * rms_norm(p[i] @ w_ple_proj[i], ple_out_norm[i])
    return x


_drawn_inputs = setup_inputs


def setup_inputs(seed=0):
    import zlib

    import numpy as np

    out = dict(_drawn_inputs(seed))
    spreads = {}
    factors = {'swa_sinks': 8.0,
     'b_router_group': 51.511,
     'b_router_expert': 5.329,
     'ple_norm': 8.0,
     'ple_out_norm': 3.229}
    for name, (base, spread) in spreads.items():
        noise = np.random.default_rng([zlib.crc32(name.encode()), seed]).standard_normal(out[name].shape)
        drawn = base * np.exp(spread * noise) if base else spread * noise
        out[name] = __import__('jax').numpy.asarray(drawn.astype(out[name].dtype))
    for name, factor in factors.items():
        out[name] = (out[name] * factor).astype(out[name].dtype)
    return out
```

```python
from contextlib import ExitStack
import math

import numpy as np
import concourse.bass as bass
from concourse import mybir

F32 = mybir.dt.float32
I32 = mybir.dt.int32
ALU = mybir.AluOpType
ACT = mybir.ActivationFunctionType
AX = mybir.AxisListType.X

P = 128
HD = 64
NEG = -1e30
EPS = 1e-6
WINDOW = 128
SLOTS = 64
BUCKETS = 32
TOEP = 384


def bucket_one_hot():
    dist = np.arange(TOEP) - 127
    n = np.maximum(dist, 0)
    exact = BUCKETS // 2
    large = exact + (np.log(np.maximum(n, 1).astype(np.float32) / exact)
                     / math.log(128 / exact) * (BUCKETS - exact)).astype(np.int32)
    bucket = np.where(n < exact, n, np.minimum(large, BUCKETS - 1))
    table = np.zeros((BUCKETS + 1, 2, TOEP), np.float32)
    for g, seen in enumerate([(dist >= 0) & (dist < WINDOW), dist >= 0]):
        table[bucket[seen], g, np.arange(TOEP)[seen]] = 1.0
        table[BUCKETS, g, ~seen] = NEG
    return table


def build_program(nc, t, out):
    x, p = t["x"][0], t["p"][0, 0]
    T, D = x.shape
    NT = T // P
    KD = D // P
    IN_W = t["w_in"].shape[2]
    NQKV = IN_W // 512
    G = t["w_router_group"].shape[2]
    E = t["w_router_expert"].shape[2]
    EG = E // G
    F = t["w_exp_gate"].shape[3]
    MF = F // P
    PD = p.shape[1]
    KP = PD // P
    PAIRS = E // 2
    RING = 12
    SLOT = 2048
    ROUNDS_MAX = T // SLOTS
    assert NT == 2 and KD == 8 and IN_W == 1536 and F == 512 and RING * SLOT == 2 * 3 * KD * F

    scratch = nc.dram_tensor("bias_scratch", (16, TOEP), F32, kind="Internal")
    ctx = ExitStack()
    with ctx:
        def sb(name, shape, dt=F32):
            return ctx.enter_context(nc.sbuf_tensor(name, shape, dt))

        def sem(name):
            return ctx.enter_context(nc.semaphore(name))

        ring = sb("ring", [P, RING, SLOT])
        w_in_sb = ring[:, RING // 2:RING, :].rearrange("p s c -> p (s c)").rearrange("p (k n) -> p k n", k=KD)
        wo_space = sb("wo_space", [P, 8192])
        w_out_sb = wo_space[:, :].rearrange("p (k n) -> p k n", k=KD)
        pg_space = sb("pg_space", [P, 8192])
        w_pg = pg_space[:, :].rearrange("p (k n) -> p k n", k=KD)
        bias = pg_space[:, 0:4096].rearrange("p (h c) -> p h c", h=16)
        S_buf = pg_space[:, 4096:6144].rearrange("p (b c) -> p b c", b=2)
        hT = S_buf
        PT_buf = pg_space[:, 6144:8192].rearrange("p (b c) -> p b c", b=2)
        sq = pg_space[:, 6144:6144 + IN_W]

        xo_space = sb("xo_space", [P, 2, 1024])
        xT = [xo_space[:, j, :].rearrange("p (k t) -> p k t", k=KD) for j in range(NT)]
        o_sb = [xo_space[:, j, :] for j in range(NT)]
        PL = xo_space
        qn_space = sb("qn_space", [P, 2, 1024])
        qn = qn_space[:, :, :].rearrange("p a c -> p (a c)")[:, 0:1280].rearrange("p (b c) -> p b c", b=10)
        v_head = qn_space[0:8, 0, 0:2 * TOEP].rearrange("p (g m) -> p g m", g=2)
        ffn_row, ple_row = qn_space[0:1, 1, :], qn_space[0:1, 0, :]
        oT = [qn_space[:, j, :].rearrange("p (k t) -> p k t", k=KD) for j in range(NT)]
        qh_space = sb("qh_space", [P, 2, 1024])
        qT = [qh_space[:, j, :].rearrange("p (g i t) -> p g i t", g=2, i=4) for j in range(NT)]
        one_hot = qh_space[0:BUCKETS + 1, 0, 0:2 * TOEP].rearrange("p (g m) -> p g m", g=2)
        h = qh_space
        kT_space = sb("kT_space", [P, 512])
        kT = kT_space[:, :].rearrange("p (g t) -> p g t", g=2)
        p_sb = kT_space[:, :].rearrange("p (j c) -> p j c", j=NT)
        v_space = sb("v_space", [P, 512])
        v_sb = v_space[:, :].rearrange("p (j g c) -> p j g c", j=NT, g=2)
        pT = v_space[:, :].rearrange("p (k t) -> p k t", k=KP)
        xs = sb("xs", [P, NT, D])
        gB = sb("gB", [P, D])

        xTe = wo_space[:, 0:1024].rearrange("p (k s) -> p k s", k=KD)
        y_sb = wo_space[:, 1024:2048]
        swT = wo_space[:, 2048:2304]
        silu = wo_space[:, 2304:2816]
        act = wo_space[:, 2816:3328]
        actT = wo_space[:, 3328:3840].rearrange("p (m s) -> p m s", m=MF)
        sel = wo_space[:, 4352:4608].rearrange("p (j e s) -> p j e s", j=NT, e=2)
        selw = wo_space[:, 4608:4864].rearrange("p (j e s) -> p j e s", j=NT, e=2)
        w_pp = wo_space[:, 4864:6912].rearrange("p (k n) -> p k n", k=KP)
        junk = wo_space[:, 6912:7424]
        key = wo_space[:, 7424:7680].rearrange("p (j r e) -> p j r e", j=NT, r=ROUNDS_MAX)

        xfT = ring[:, 0, :].rearrange("p (j k t) -> p j k t", j=NT, k=KD)
        gate = ring[:, 1, :].rearrange("p (j c) -> p j c", j=NT)
        result = ring[:, 2, :].rearrange("p (j c) -> p j c", j=NT)

        ident = sb("ident", [P, P])
        before = sb("before", [P, P])
        ones = sb("ones", [P, P])
        iota = sb("iota", [P, SLOTS])
        first = sb("first", [P, E])
        neghalf = sb("neghalf", [P, 24])
        gain_rows = sb("gain_rows", [28, P])
        gT = sb("gT", [P, 28])
        tbl = sb("tbl", [BUCKETS + 1, 16])
        sinks = sb("sinks", [P, 8])
        r_bias = sb("r_bias", [P, G + E])
        w_r = sb("w_r", [P, KD, G + E])
        st = sb("st", [P, 64])
        ss_h = sb("ss_h", [P, 24])
        f_h = sb("f_h", [P, 24])
        mx = sb("mx", [P, 2, 16])
        negm = sb("negm", [P, 2, 16])
        rsum = sb("rsum", [P, 2, 16])
        snk = sb("snk", [P, 2, 8])
        snk_e = sb("snk_e", [P, 2, 8])
        rden = sb("rden", [P, 2, 16])
        lg = sb("lg", [P, NT, G + E])
        ra = sb("ra", [P, 2, E])
        rb = sb("rb", [P, E])
        em = sb("em", [P, E])
        rs = sb("rs", [P, 2, 16])
        member = sb("member", [P, NT, E])
        weight = sb("weight", [P, NT, ROUNDS_MAX, E])
        counts = sb("counts", [P, 4])
        n_i = sb("n_i", [P, 4], I32)

        bank = ctx.enter_context(nc.psum_tensor("bank", [P, 8, 512], F32))

        x_in = [sem(f"x_in{j}") for j in range(NT)]
        win_in = [sem(f"win_in{k}") for k in range(KD)]
        wout_in = [sem(f"wout_in{k}") for k in range(4)]
        slot_in = [sem(f"slot_in{s}") for s in range(RING)]
        wpg_in, wpp_in, p_in = sem("wpg_in"), sem("wpp_in"), sem("p_in")
        gain_in, tbl_in, route_in = sem("gain_in"), sem("tbl_in"), sem("route_in")
        scr_out, bias_in, out_done = sem("scr_out"), sem("bias_in"), sem("out_done")
        consts, pool_chain, mask_row = sem("consts"), sem("pool_chain"), sem("mask_row")
        setup_mm, v_ready, gT_ready, gB_ready = sem("setup_mm"), sem("v_ready"), sem("gT_ready"), sem("gB_ready")
        xt_mm, xt_ready = sem("xt_mm"), sem("xt_ready")
        stat_v, stat_r, sum_ready = sem("stat_v"), sem("stat_r"), sem("sum_ready")
        qkv_mm, sq_ready, ssh_ready, qn_ready, v_copied = (sem(n) for n in (
            "qkv_mm", "sq_ready", "ssh_ready", "qn_ready", "v_copied"))
        qt_mm, qta_ready, qtb_ready = sem("qt_mm"), sem("qta_ready"), sem("qtb_ready")
        s_mm, s_added, m_ready, exp_done, snk_ready, snk_exp = (sem(n) for n in (
            "s_mm", "s_added", "m_ready", "exp_done", "snk_ready", "snk_exp"))
        pt_mm, pt_ready, pv_mm, o_ready, oss_ready, on_ready = (sem(n) for n in (
            "pt_mm", "pt_ready", "pv_mm", "o_ready", "oss_ready", "on_ready"))
        ot_mm, ot_ready, proj_mm, x1_ready, h_ready, ht_mm, ht_ready, logit_mm = (sem(n) for n in (
            "ot_mm", "ot_ready", "proj_mm", "x1_ready", "h_ready", "ht_mm", "ht_ready", "logit_mm"))
        r_max, r_exp, member_ready, rank_mm, key_ready, n_ready = (sem(n) for n in (
            "r_max", "r_exp", "member_ready", "rank_mm", "key_ready", "n_ready"))
        dve_step = sem("dve_step")
        slots_read = sem("slots_read")
        sel_ready, selw_ready, gather_mm, xte_ready = (sem(n) for n in (
            "sel_ready", "selw_ready", "gather_mm", "xte_ready"))
        silu_ready, act_ready, act_mm, actt_ready, y0_ready, y1_ready = (sem(n) for n in (
            "silu_ready", "act_ready", "act_mm", "actt_ready", "y0_ready", "y1_ready"))
        swt_mm, swt_ready, mix_mm, mix_added = (sem(n) for n in ("swt_mm", "swt_ready", "mix_mm", "mix_added"))
        pp_mm, pp_out, pp_var, pp_root, wpg_scaled = (sem(n) for n in ("pp_mm", "pp_out", "pp_var", "pp_root", "wpg_scaled"))
        xf_mm, xfa_ready, xfb_ready, gate_mm, gate_ready, res_ready = (sem(n) for n in (
            "xf_mm", "xfa_ready", "xfb_ready", "gate_mm", "gate_ready", "res_ready"))

        w_g, w_u, w_d = t["w_exp_gate"][0], t["w_exp_up"][0], t["w_exp_down"][0]

        def expert_slot(pair, s):
            part, half, e = s // 4, (s % 4) // 2, s % 2
            w = (w_g, w_u, w_d)[part]
            rows = w.shape[1] // 2
            v = w.rearrange("(i two) (s r) n -> i two s r n", two=2, s=2)
            v = v[bass.ds(pair, 1), e, half]
            return v.rearrange("i (k p) n -> p (i k) n", p=P)

        def slot_dst(s):
            k = 2 if s // 4 == 2 else 4
            return ring[:, s, :].rearrange("p (k n) -> p k n", k=k)

        def lg_of(j):
            return lg[:, j, :]

        S0_BANKS = [1, 2, 6, 0]
        S1_BANKS = [0, 3, 0, 3]

        block = ctx.enter_context(nc.Block())

        @block.sync
        def _(sp):
            for j in range(NT):
                sp.dma_start(xs[:, j, :], x[j * P:(j + 1) * P, :]).then_inc(x_in[j], 16)
            for k in range(KD):
                sp.dma_start(w_in_sb[:, k, :], t["w_in"][0, k * P:(k + 1) * P, :]).then_inc(win_in[k], 16)
            wo = t["w_out"][0].rearrange("(q k p) n -> q p k n", k=2, p=P)
            for q in range(4):
                sp.dma_start(w_out_sb[:, 2 * q:2 * q + 2, :], wo[q]).then_inc(wout_in[q], 16)
            for s in range(RING):
                if s == RING // 2:
                    sp.wait_ge(qkv_mm, 2)
                sp.dma_start(slot_dst(s), expert_slot(0, s)).then_inc(slot_in[s], 16)
            sp.wait_ge(logit_mm, 2)
            sp.dma_start(p_sb, p.rearrange("(j p) c -> p j c", p=P)).then_inc(p_in, 16)
            sp.dma_start(ple_row, t["ple_out_norm"]).then_inc(p_in, 16)
            sp.dma_start(w_pp, t["w_ple_proj"][0].rearrange("(k p) n -> p k n", p=P)).then_inc(wpp_in, 16)
            sp.dma_start(w_pg, t["w_ple_gate"][0].rearrange("(k p) n -> p k n", p=P)).then_inc(wpg_in, 16)

            def pair_loads(previous, pair):
                for s in range(RING):
                    sp.wait_ge(slots_read, RING * previous + (s + 1))
                    sp.dma_start(slot_dst(s), expert_slot(pair, s)).then_inc(slot_in[s], 16)

            with sp.Fori(0, PAIRS - 1) as previous:
                pair_loads(previous, previous + 1)
            sp.wait_ge(n_ready, 1)
            more = sp.value_load(n_i[0:1, 3:4], min_val=0, max_val=ROUNDS_MAX - 1)
            with sp.If(more > 0):
                with sp.Fori(0, more) as r:
                    with sp.Fori(0, PAIRS) as pair:
                        pair_loads(r * PAIRS + pair + (PAIRS - 1), pair)
            for j in range(NT):
                for n in range(2):
                    sp.wait_ge(res_ready, 2 * j + n + 1)
                    sp.dma_start(out[0, j * P:(j + 1) * P, n * 512:(n + 1) * 512],
                                 result[:, j, n * 512:(n + 1) * 512]).then_inc(out_done, 16)
            sp.wait_ge(out_done, 16 * 2 * NT)

        @block.gpsimd
        def _(pool):
            chain = [0]

            def link(ins):
                chain[0] += 1
                ins.then_inc(pool_chain, 1)
                pool.wait_ge(pool_chain, chain[0])

            link(pool.memset(ident[:, :], 0.0))
            link(pool.affine_select(out=ident[:, :], in_=ident[:, :], compare_op=ALU.not_equal, fill=1.0,
                                    base=0, pattern=[[-1, P]], channel_multiplier=1))
            link(pool.memset(ones[:, :], 1.0))
            pool.affine_select(out=before[:, :], in_=ones[:, :], compare_op=ALU.is_gt, fill=0.0,
                               base=0, pattern=[[1, P]], channel_multiplier=-1).then_inc(consts, 1)
            pool.iota(iota[:, :], [[1, SLOTS]], base=0, channel_multiplier=0,
                      allow_small_or_imprecise_dtypes=True).then_inc(consts, 1)
            pool.iota(first[:, :], [[-1, E]], base=E, channel_multiplier=0,
                      allow_small_or_imprecise_dtypes=True).then_inc(consts, 1)
            link(pool.memset(neghalf[:, :], -0.5))

            def rsqrt(n, dst, src):
                pool.wait_ge(stat_v, n)
                pool.tensor_tensor(dst, src, neghalf[:, 0:dst.shape[1]], ALU.pow).then_inc(stat_r, 1)

            rsqrt(1, st[:, 2:4], st[:, 2:4])
            rsqrt(2, f_h[:, :], ss_h[:, :])
            rsqrt(3, f_h[:, :], ss_h[:, :])
            rsqrt(4, st[:, 10:12], st[:, 10:12])
            rsqrt(5, st[:, 20:21], st[:, 20:21])
            rsqrt(6, st[:, 12:14], st[:, 12:14])
            rsqrt(7, st[:, 21:22], st[:, 21:22])

            pool.wait_ge(wpg_in, 16)
            for k in range(KD):
                pool.tensor_scalar(w_pg[:, k, :], w_pg[:, k, :], gT[:, 8 + k:9 + k], 1.0,
                                   ALU.mult, ALU.mult).then_inc(wpg_scaled, 1)
            rsqrt(8, st[:, 52:53], st[:, 50:51])
            rsqrt(9, st[:, 53:54], st[:, 51:52])

        @block.tensor
        def _(pe):
            pe.wait_ge(consts, 3)
            pe.wait_ge(pool_chain, 3)
            pe.wait_ge(gain_in, 16 * 13)
            pe.transpose(bank[:, 7, 0:28], gain_rows[:, :], ident[0:28, 0:28]).then_inc(setup_mm, 1)
            pe.wait_ge(tbl_in, 32)
            pe.wait_ge(mask_row, 1)
            for g in range(2):
                pe.matmul(bank[0:8, 5 + g, 0:TOEP], tbl[:, 8 * g:8 * g + 8], one_hot[:, g, :],
                          start=True, stop=True).then_inc(setup_mm, 1)
            for n in range(2):
                pe.matmul(bank[:, 3 + n, :], ones[0:1, :], ffn_row[:, n * 512:(n + 1) * 512],
                          start=True, stop=True).then_inc(setup_mm, 1)

            pe.wait_ge(gT_ready, 1)
            pe.wait_ge(v_ready, 2)
            for j in range(NT):
                pe.wait_ge(x_in[j], 16)
                for b in range(2):
                    if j:
                        pe.wait_ge(xt_ready, b + 1)
                    for k in range(4):
                        mm = pe.transpose(bank[:, 6 + b, k * P:(k + 1) * P],
                                          xs[:, j, (4 * b + k) * P:(4 * b + k + 1) * P], ident[:, :])
                    mm.then_inc(xt_mm, 1)

            pe.wait_ge(gB_ready, 2)
            for j in range(NT):
                pe.wait_ge(xt_ready, 2 * j + 2)
                for k in range(KD):
                    if j == 0:
                        pe.wait_ge(win_in[k], 16)
                    for n in range(NQKV):
                        mm = pe.matmul(bank[:, 3 * j + n, :], xT[j][:, k, :], w_in_sb[:, k, n * 512:(n + 1) * 512],
                                       start=(k == 0), stop=(k == KD - 1))
                mm.then_inc(qkv_mm, 1)

            def qk_transposes(j, banks):
                pe.wait_ge(qn_ready, 5 * (j + 1))
                for b, blocks in zip(banks, ([0, 1, 2, 3], [5, 6, 7, 8], [4, 9])):
                    for n, blk in enumerate(blocks):
                        mm = pe.transpose(bank[:, b, n * P:(n + 1) * P], qn[:, blk, :], ident[:, :])
                    mm.then_inc(qt_mm, 1)

            def scores(j, c):
                g, u = c // 2, c % 2
                rows = slice(u * HD, (u + 1) * HD)
                W = (j + 1) * P
                for i in range(4):
                    if j == 0:
                        dst = bank[:, S0_BANKS[c], i * P:(i + 1) * P]
                    else:
                        dst = bank[:, S1_BANKS[c] + i // 2, (i % 2) * W:(i % 2 + 1) * W]
                    mm = pe.matmul(dst, qT[j][rows, g, i, :], kT[rows, g, 0:W], start=True, stop=True)
                mm.then_inc(s_mm, 1)

            def probs_v(j, c, o_banks):
                g, u = c // 2, c % 2
                n = 4 * j + c
                W = (j + 1) * P
                pe.wait_ge(exp_done, 4 * n + 4)
                if n:
                    pe.wait_ge(pt_ready, c if j == 0 else 4 + 2 * c)
                src = S_buf[:, n % 2, 0:4 * W].rearrange("p (i w) -> p i w", i=4)
                for i in range(4):
                    for kb in range(j + 1):
                        m = i * (j + 1) + kb
                        mm = pe.transpose(bank[:, [7, 5][m // 4], (m % 4) * P:(m % 4 + 1) * P],
                                          src[:, i, kb * P:(kb + 1) * P], ident[:, :])
                        if m % 4 == 3:
                            mm.then_inc(pt_mm, 1)
                pe.wait_ge(pt_ready, c + 1 if j == 0 else 4 + 2 * c + 2)
                dst = bank[:, o_banks[g], :].rearrange("p (h d) -> p h d", d=HD)
                probs = PT_buf[:, n % 2, 0:4 * W].rearrange("p (i w) -> p i w", i=4)
                for i in range(4):
                    for kb in range(j + 1):
                        mm = pe.matmul(dst[:, 4 * u + i, :], probs[:, i, kb * P:(kb + 1) * P],
                                       v_sb[:, kb, g, u * HD:(u + 1) * HD], start=(kb == 0), stop=(kb == j))
                mm.then_inc(pv_mm, 1)

            def o_transposes(j):
                for b in range(2):
                    pe.wait_ge(on_ready, 2 * j + b + 1)
                    for k in range(4):
                        mm = pe.transpose(bank[:, [7, 5][b], k * P:(k + 1) * P],
                                          o_sb[j][:, (4 * b + k) * P:(4 * b + k + 1) * P], ident[:, :])
                    mm.then_inc(ot_mm, 1)

            def out_projection(j):
                pe.wait_ge(ot_ready, 2 * j + 2)
                for n in range(2):
                    for k in range(KD):
                        if j == 0 and n == 0 and k % 2 == 0:
                            pe.wait_ge(wout_in[k // 2], 16)
                        mm = pe.matmul(bank[:, [2, 6][n], :], oT[j][:, k, :], w_out_sb[:, k, n * 512:(n + 1) * 512],
                                       start=(k == 0), stop=(k == KD - 1))
                    mm.then_inc(proj_mm, 1)

            def logits(j):
                for b in range(2):
                    pe.wait_ge(h_ready, j + 1)
                    if j:
                        pe.wait_ge(ht_ready, b + 1)
                    for k in range(4):
                        mm = pe.transpose(bank[:, b, k * P:(k + 1) * P],
                                          h[:, j, (4 * b + k) * P:(4 * b + k + 1) * P], ident[:, :])
                    mm.then_inc(ht_mm, 1)
                pe.wait_ge(ht_ready, 2 * j + 2)
                pe.wait_ge(route_in, 16 * 5)
                for k in range(KD):
                    mm = pe.matmul(bank[:, 3 + j, 0:G + E], hT[:, j, k * P:(k + 1) * P], w_r[:, k, :],
                                   start=(k == 0), stop=(k == KD - 1))
                mm.then_inc(logit_mm, 1)

            qk_transposes(0, (6, 7, 0))
            pe.wait_ge(qta_ready, 1)
            pe.wait_ge(qtb_ready, 3)
            pe.wait_ge(v_copied, 2)
            for c in range(4):
                scores(0, c)
            pe.wait_ge(qn_ready, 10)
            pe.wait_ge(v_copied, 4)
            for c in range(4):
                probs_v(0, c, (3, 4))
            qk_transposes(1, (1, 2, 6))
            pe.wait_ge(qta_ready, 2)
            pe.wait_ge(qtb_ready, 6)
            scores(1, 0)
            pe.wait_ge(o_ready, 2)
            scores(1, 1)
            o_transposes(0)
            out_projection(0)
            probs_o = (2, 6)
            pe.wait_ge(x1_ready, 2)
            for c in range(4):
                probs_v(1, c, probs_o)
                if c < 2:
                    scores(1, c + 2)
            logits(0)
            o_transposes(1)
            out_projection(1)
            logits(1)

            pe.wait_ge(member_ready, 2)
            pe.matmul(bank[:, 5, 0:E], before[:, :], member[:, 0, :], start=True, stop=True)
            pe.matmul(bank[:, 5, E:2 * E], before[:, :], member[:, 1, :], start=True, stop=False)
            pe.matmul(bank[:, 5, E:2 * E], ones[:, :], member[:, 0, :], start=False, stop=True)
            pe.matmul(bank[:, 5, 2 * E:3 * E], ones[:, :], member[:, 0, :], start=True, stop=False)
            pe.matmul(bank[:, 5, 2 * E:3 * E], ones[:, :], member[:, 1, :], start=False,
                      stop=True).then_inc(rank_mm, 1)

            def gather(i, b):
                if b == 0:
                    pe.wait_ge(sel_ready, i + 1)
                for k in range(4 * b, 4 * b + 4):
                    for j in range(NT):
                        mm = pe.matmul(bank[:, b, (k % 4) * P:(k % 4 + 1) * P], h[:, j, k * P:(k + 1) * P],
                                       sel[:, j, :, :].rearrange("p e s -> p (e s)"),
                                       start=(j == 0), stop=(j == NT - 1))
                mm.then_inc(gather_mm, 1)

            def weights(i, part, half, e):
                s = 4 * part + 2 * half + e
                pe.wait_ge(slot_in[s], 16 * i + 16)
                return ring[:, s, :].rearrange("p (k n) -> p k n", k=2 if part == 2 else 4)

            def gate_or_up(i, part):
                for half in range(2):
                    w = [weights(i, part, half, e) for e in range(2)]
                    for k in range(4):
                        for e in range(2):
                            mm = pe.matmul(bank[e * SLOTS:(e + 1) * SLOTS, 2 + part, :],
                                           xTe[:, 4 * half + k, e * SLOTS:(e + 1) * SLOTS], w[e][:, k, :],
                                           start=(half == 0 and k == 0), stop=(half == 1 and k == 3))
                            if k == 3:
                                mm.then_inc(slots_read, 1)

            def down(i):
                pe.wait_ge(actt_ready, i + 1)
                for half in range(2):
                    w = [weights(i, 2, half, e) for e in range(2)]
                    for n in range(2):
                        for m in range(2):
                            for e in range(2):
                                mm = pe.matmul(bank[e * SLOTS:(e + 1) * SLOTS, 6 + n, :],
                                               actT[:, 2 * half + m, e * SLOTS:(e + 1) * SLOTS],
                                               w[e][:, m, n * 512:(n + 1) * 512],
                                               start=(half == 0 and m == 0), stop=(half == 1 and m == 1))
                                if n == 1 and m == 1:
                                    mm.then_inc(slots_read, 1)

            def act_transposes(i):
                pe.wait_ge(act_ready, i + 1)
                for m in range(MF):
                    mm = pe.transpose(bank[:, 4, m * P:(m + 1) * P], act[:, m * P:(m + 1) * P], ident[:, :])
                mm.then_inc(act_mm, 1)

            def weight_transposes(i):
                pe.wait_ge(selw_ready, i + 1)
                for j in range(NT):
                    mm = pe.transpose(bank[:, 5, j * P:(j + 1) * P],
                                      selw[:, j, :, :].rearrange("p e s -> p (e s)"), ident[:, :])
                mm.then_inc(swt_mm, 1)

            def mix(i, j):
                if j == 0:
                    pe.wait_ge(y0_ready, i + 1)
                    pe.wait_ge(y1_ready, i + 1)
                    pe.wait_ge(swt_ready, i + 1)
                for n in range(2):
                    pe.matmul(bank[:, 4 * j + n, :], swT[:, j * P:(j + 1) * P], y_sb[:, n * 512:(n + 1) * 512],
                              start=True, stop=True).then_inc(mix_mm, 1)

            def project_p():
                pe.wait_ge(swt_ready, 1)
                pe.wait_ge(n_ready, 1)
                pe.wait_ge(p_in, 32)
                for k in range(KP):
                    for j in range(NT):
                        mm = pe.transpose(bank[:, 4, (2 * k + j) * P:(2 * k + j + 1) * P],
                                          p_sb[:, j, k * P:(k + 1) * P], ident[:, :])
                mm.then_inc(pp_mm, 1)
                for n in range(2):
                    if n:
                        pe.wait_ge(pp_out, 1)
                    pe.matmul(bank[:, 5 - n, :], ones[0:1, :], ple_row[:, n * 512:(n + 1) * 512],
                              start=True, stop=True).then_inc(pp_mm, 1)
                pe.wait_ge(wpp_in, 16)
                for j in range(NT):
                    for n in range(2):
                        pe.wait_ge(pp_out, 2 + 2 * j + n)
                        for k in range(KP):
                            mm = pe.matmul(bank[:, 5 - n, :], pT[:, k, j * P:(j + 1) * P],
                                           w_pp[:, k, n * 512:(n + 1) * 512], start=(k == 0), stop=(k == KP - 1))
                        mm.then_inc(pp_mm, 1)

            def pair_step(previous, has_next):
                i = 0 if previous is None else previous + 1
                pe.wait_ge(xte_ready, 2 * i + 2)
                if previous is not None:
                    pe.wait_ge(act_ready, previous + 1)
                gate_or_up(i, 0)
                if previous is not None:
                    mix(previous, 0)
                gate_or_up(i, 1)
                if previous is not None:
                    pe.wait_ge(mix_added, 4 * previous + 4)
                    mix(previous, 1)
                    pe.wait_ge(mix_added, 4 * previous + 6)
                if has_next:
                    gather(i + 1, 0)
                if previous is not None:
                    pe.wait_ge(mix_added, 4 * previous + 7)
                act_transposes(i)
                if has_next:
                    gather(i + 1, 1)
                if previous is not None:
                    pe.wait_ge(mix_added, 4 * previous + 8)
                weight_transposes(i)
                if previous is not None:
                    pe.wait_ge(y0_ready, previous + 1)
                    pe.wait_ge(y1_ready, previous + 1)
                down(i)

            gather(0, 0)
            gather(0, 1)
            pair_step(None, True)
            project_p()
            before_last = pe.value_load(n_i[0:1, 2:3], min_val=PAIRS - 2, max_val=PAIRS * ROUNDS_MAX - 2)
            n_pairs = pe.value_load(n_i[0:1, 0:1], min_val=PAIRS, max_val=PAIRS * ROUNDS_MAX)
            with pe.Fori(0, before_last) as previous:
                pair_step(previous, True)
            pair_step(before_last, False)
            for j in range(NT):
                mix(before_last + 1, j)

            for j in range(NT):
                pe.wait_ge(mix_added, 4 * n_pairs + 2 * (j + 1))
                for b in range(2):
                    for k in range(4):
                        mm = pe.transpose(bank[:, 2 - 2 * j + b, k * P:(k + 1) * P],
                                          xs[:, j, (4 * b + k) * P:(4 * b + k + 1) * P], ident[:, :])
                    mm.then_inc(xf_mm, 1)
            pe.wait_ge(wpg_scaled, KD)
            for j in range(NT):
                pe.wait_ge(xfa_ready, j + 1)
                pe.wait_ge(xfb_ready, j + 1)
                for n in range(2):
                    for k in range(KD):
                        mm = pe.matmul(bank[:, 6 - 2 * j + n, :], xfT[:, j, k, :], w_pg[:, k, n * 512:(n + 1) * 512],
                                       start=(k == 0), stop=(k == KD - 1))
                    mm.then_inc(gate_mm, 1)

        @block.scalar
        def _(actv):
            ACTF = nc.scalar.activation

            def small(dst, src, s):
                actv.dma_start(dst, src).then_inc(s, 16)

            rows = lambda a: a.rearrange("(r c) -> r c", c=P)
            small(gain_rows[0:8, :], rows(t["attn_norm"][0]), gain_in)
            small(gain_rows[8:16, :], rows(t["ple_norm"][0]), gain_in)
            small(gain_rows[16:20, :], rows(t["swa_out_norm"][0]), gain_in)
            small(gain_rows[20:24, :], rows(t["moba_out_norm"][0]), gain_in)
            for n, name in enumerate(["swa_q_norm", "swa_k_norm", "moba_q_norm", "moba_k_norm"]):
                for u in range(2):
                    small(gain_rows[24 + n:25 + n, u * HD:(u + 1) * HD], t[name], gain_in)
            small(ffn_row, t["ffn_norm"], gain_in)
            small(tbl[0:BUCKETS, :], t["rel_bias"], tbl_in)
            small(one_hot, t["bucket_one_hot"], tbl_in)
            small(w_r[:, :, 0:G], t["w_router_group"][0].rearrange("(k p) g -> p k g", p=P), route_in)
            small(w_r[:, :, G:G + E], t["w_router_expert"][0].rearrange("(k p) g -> p k g", p=P), route_in)
            small(r_bias[:, 0:G], t["b_router_group"].partition_broadcast(P).rearrange("q a c -> q (a c)"), route_in)
            small(r_bias[:, G:G + E], t["b_router_expert"].partition_broadcast(P).rearrange("q a c -> q (a c)"), route_in)
            small(sinks[:, :], t["swa_sinks"].partition_broadcast(P).rearrange("q a c -> q (a c)"), route_in)

            actv.wait_ge(setup_mm, 3)
            for g in range(2):
                actv.copy(v_head[:, g, :], bank[0:8, 5 + g, 0:TOEP]).then_inc(v_ready, 1)
            actv.wait_ge(v_ready, 2)
            actv.dma_start(scratch.ap().rearrange("(g h) m -> h g m", g=2), v_head).then_inc(scr_out, 16)
            actv.wait_ge(scr_out, 16)
            toeplitz = bass.AP(scratch, 0, [[1, P], [TOEP, 16], [1, 2 * P]])
            actv.dma_start(bias, toeplitz).then_inc(bias_in, 16)
            for n in range(2):
                actv.wait_ge(setup_mm, 4 + n)
                actv.copy(gB[:, n * 512:(n + 1) * 512], bank[:, 3 + n, :]).then_inc(gB_ready, 1)

            for j in range(NT):
                actv.wait_ge(x_in[j], 16)
                ACTF(sq[:, 0:D], xs[:, j, :], ACT.Square, accum_out=st[:, j:j + 1]).then_inc(sum_ready, 1)
                actv.wait_ge(sum_ready, j + 1)

            def squares(j):
                actv.wait_ge(qkv_mm, j + 1)
                actv.wait_ge(stat_r, 1)
                if j:
                    actv.wait_ge(ssh_ready, 1)
                for n in range(NQKV):
                    ACTF(sq[:, n * 512:(n + 1) * 512], bank[:, 3 * j + n, :], ACT.Square,
                         scale=st[:, 2 + j:3 + j]).then_inc(sq_ready, 1)
                actv.mul(v_sb[:, j, 0, :], bank[:, 3 * j + 1, 128:256], st[:, 2 + j:3 + j]).then_inc(v_copied, 1)
                actv.mul(v_sb[:, j, 1, :], bank[:, 3 * j + 2, 384:512], st[:, 2 + j:3 + j]).then_inc(v_copied, 1)

            def q_columns(j, b0):
                actv.wait_ge(qt_mm, 3 * j + 1)
                actv.mul(qT[j][:, 0, :, :].rearrange("p i t -> p (i t)"), bank[:, b0, :],
                         gT[:, 24:25]).then_inc(qta_ready, 1)

            def exps(j, c):
                n = 4 * j + c
                W = (j + 1) * P
                actv.wait_ge(m_ready, n + 1)
                for i in range(4):
                    hh = 4 * c + i
                    s = S_buf[:, n % 2, i * W:(i + 1) * W]
                    ACTF(s, s, ACT.Exp, bias=negm[:, j, hh:hh + 1], accum_out=rsum[:, j, hh:hh + 1]).then_inc(exp_done, 1)
                if c < 2:
                    actv.wait_ge(snk_ready, 2 * j + c + 1)
                    ACTF(snk_e[:, j, 4 * c:4 * c + 4], snk[:, j, 4 * c:4 * c + 4], ACT.Exp).then_inc(snk_exp, 1)

            def prob_columns(j, c):
                n = 4 * j + c
                for b in range(j + 1):
                    done = c + 1 if j == 0 else 4 + 2 * c + b + 1
                    actv.wait_ge(pt_mm, done)
                    if n == 0:
                        actv.wait_ge(ssh_ready, 2)
                    actv.copy(PT_buf[:, n % 2, b * 512:(b + 1) * 512], bank[:, [7, 5][b], :]).then_inc(pt_ready, 1)

            def o_squares(j):
                actv.wait_ge(o_ready, 2 * j + 2)
                for g in range(2):
                    ACTF(qh_space[:, j, g * 512:(g + 1) * 512], o_sb[j][:, g * 512:(g + 1) * 512], ACT.Square,
                         accum_out=st[:, 30 + 2 * j + g:31 + 2 * j + g]).then_inc(oss_ready, 1)

            def x_squares(j):
                actv.wait_ge(x1_ready, 2 * j + 2)
                actv.wait_ge(oss_ready, 2 * j + 2)
                ACTF(qh_space[:, j, :], xs[:, j, :], ACT.Square, accum_out=st[:, 34 + j:35 + j]).then_inc(sum_ready, 1)

            def h_columns(j):
                for b in range(2):
                    actv.wait_ge(ht_mm, 2 * j + b + 1)
                    actv.copy(hT[:, j, b * 512:(b + 1) * 512], bank[:, b, :]).then_inc(ht_ready, 1)

            squares(0)
            squares(1)
            q_columns(0, 6)
            for c in range(4):
                exps(0, c)
                prob_columns(0, c)
            q_columns(1, 1)
            o_squares(0)
            exps(1, 0)
            exps(1, 1)
            prob_columns(1, 0)
            x_squares(0)
            exps(1, 2)
            prob_columns(1, 1)
            exps(1, 3)
            prob_columns(1, 2)
            prob_columns(1, 3)
            h_columns(0)
            o_squares(1)

            def route_exps(j):
                actv.wait_ge(r_max, 2 * j + 1)
                ACTF(rs[:, j, 4:8], lg_of(j)[:, 0:G], ACT.Exp, bias=rs[:, j, 1:2],
                     accum_out=rs[:, j, 8:9]).then_inc(r_exp, 1)
                actv.wait_ge(r_max, 2 * j + 2)
                ACTF(rs[:, j, 9:10], rs[:, j, 3:4], ACT.Exp, bias=rs[:, j, 10:11]).then_inc(r_exp, 1)

            route_exps(0)
            x_squares(1)
            h_columns(1)
            route_exps(1)

            def tokens_in(i, b):
                actv.wait_ge(gather_mm, 2 * i + (b + 1))
                actv.copy(xTe[:, 4 * b:4 * b + 4, :].rearrange("p k s -> p (k s)"),
                          bank[:, b, :]).then_inc(xte_ready, 1)

            def pair_step(previous, has_next):
                i = 0 if previous is None else previous + 1
                actv.wait_ge(slots_read, RING * i + 4)
                if previous is not None:
                    actv.wait_ge(act_ready, previous + 1)
                ACTF(silu, bank[:, 2, :], ACT.Silu).then_inc(silu_ready, 1)
                if has_next:
                    tokens_in(i + 1, 0)
                actv.wait_ge(act_mm, i + 1)
                actv.copy(actT.rearrange("p m s -> p (m s)"), bank[:, 4, :]).then_inc(actt_ready, 1)
                if has_next:
                    tokens_in(i + 1, 1)
                actv.wait_ge(swt_mm, i + 1)
                actv.copy(swT, bank[:, 5, 0:NT * P]).then_inc(swt_ready, 1)
                actv.wait_ge(slots_read, RING * i + 12)
                actv.copy(y_sb[:, 0:512], bank[:, 6, :]).then_inc(y0_ready, 1)

            tokens_in(0, 0)
            tokens_in(0, 1)
            pair_step(None, True)
            actv.wait_ge(pp_mm, 1)
            actv.copy(pT.rearrange("p k t -> p (k t)"), bank[:, 4, :]).then_inc(pp_out, 1)
            for n in range(2):
                actv.wait_ge(pp_mm, 2 + n)
                actv.copy(gB[:, n * 512:(n + 1) * 512], bank[:, 5 - n, :]).then_inc(pp_out, 1)
            for j in range(NT):
                for n in range(2):
                    actv.wait_ge(pp_mm, 4 + 2 * j + n)
                    actv.copy(PL[:, j, n * 512:(n + 1) * 512], bank[:, 5 - n, :])
                    actv.wait_ge(pp_out, 3 + 2 * j + n)
                    ACTF(junk, bank[:, 5 - n, :], ACT.Square,
                         accum_out=st[:, 40 + 2 * j + n:41 + 2 * j + n]).then_inc(pp_out, 1)
            actv.wait_ge(pp_var, 1)
            ACTF(st[:, 46:48], st[:, 44:46], ACT.Sqrt).then_inc(pp_root, 1)

            actv.wait_ge(n_ready, 1)
            n_pairs = actv.value_load(n_i[0:1, 0:1], min_val=PAIRS, max_val=PAIRS * ROUNDS_MAX)
            before_last = actv.value_load(n_i[0:1, 2:3], min_val=PAIRS - 2, max_val=PAIRS * ROUNDS_MAX - 2)
            with actv.Fori(0, before_last) as previous:
                pair_step(previous, True)
            pair_step(before_last, False)

            for j in range(NT):
                actv.wait_ge(xf_mm, 2 * j + 1)
                actv.copy(xfT[:, j, 0:4, :].rearrange("p k t -> p (k t)"), bank[:, 2 - 2 * j, :]).then_inc(xfa_ready, 1)
                actv.wait_ge(mix_added, 4 * n_pairs + 2 * (j + 1))
                ACTF(ring[:, 3 + j, 0:D], xs[:, j, :], ACT.Square, accum_out=st[:, 48 + j:49 + j]).then_inc(sum_ready, 1)
            for j in range(NT):
                actv.wait_ge(stat_r, 8 + j)
                for n in range(2):
                    actv.wait_ge(gate_mm, 2 * j + n + 1)
                    ACTF(gate[:, j, n * 512:(n + 1) * 512], bank[:, 6 - 2 * j + n, :], ACT.Sigmoid,
                         scale=st[:, 52 + j:53 + j]).then_inc(gate_ready, 1)

        @block.vector
        def _(dve):
            chain = [0]

            def link(ins):
                chain[0] += 1
                ins.then_inc(dve_step, 1)
                dve.wait_ge(dve_step, chain[0])

            V = nc.vector

            def cols(a, n, w):
                return a.unsqueeze(2).to_broadcast([P, n, w])

            V.memset(tbl[BUCKETS:BUCKETS + 1, :], 1.0).then_inc(mask_row, 1)
            dve.wait_ge(setup_mm, 1)
            link(V.tensor_copy(gT[:, :], bank[:, 7, 0:28]))
            for c in (24, 26):
                V.tensor_scalar(gT[:, c:c + 1], gT[:, c:c + 1], HD ** -0.5, None, ALU.mult).then_inc(dve_step, 1)
            chain[0] += 2
            dve.wait_ge(dve_step, chain[0])
            dve.sem_inc(gT_ready, 1)

            for j in range(NT):
                for b in range(2):
                    dve.wait_ge(xt_mm, 2 * j + b + 1)
                    V.tensor_tensor(xT[j][:, 4 * b:4 * b + 4, :],
                                    bank[:, 6 + b, :].rearrange("p (k t) -> p k t", k=4),
                                    cols(gT[:, 4 * b:4 * b + 4], 4, P), ALU.mult).then_inc(xt_ready, 1)
            dve.wait_ge(sum_ready, 2)
            V.tensor_scalar(st[:, 2:4], st[:, 0:2], 1.0 / D, EPS, ALU.mult, ALU.add).then_inc(stat_v, 1)

            def head_sums(j):
                dve.wait_ge(sq_ready, 3 * (j + 1))
                if j:
                    dve.wait_ge(stat_r, 2)
                link(V.tensor_reduce(ss_h[:, :], sq.rearrange("p (h d) -> p h d", d=HD), AX, ALU.add))
                V.tensor_scalar(ss_h[:, :], ss_h[:, :], 1.0 / HD, EPS, ALU.mult, ALU.add).then_inc(stat_v, 1)
                dve.sem_inc(ssh_ready, 1)

            def normed_heads(j):
                dve.wait_ge(stat_r, 2 + j)
                dve.wait_ge(v_copied, 2 * j + 2)
                link(V.tensor_scalar(f_h[:, :], f_h[:, :], st[:, 2 + j:3 + j], None, ALU.mult))
                if j:
                    dve.wait_ge(qt_mm, 3)
                else:
                    dve.wait_ge(scr_out, 16)

                def heads(b, at, h0, n, dst):
                    src = bank[:, 3 * j + b, at:at + n * HD].rearrange("p (i d) -> p i d", d=HD)
                    V.tensor_tensor(dst, src, cols(f_h[:, h0:h0 + n], n, HD), ALU.mult).then_inc(qn_ready, 1)

                pairs = qn.rearrange("p b (u d) -> p b u d", u=2)
                src = bank[:, 3 * j, :].rearrange("p (u i d) -> p u i d", u=2, d=HD)
                f = f_h[:, 0:8].rearrange("p (u i) -> p u i", u=2).unsqueeze(3).to_broadcast([P, 2, 4, HD])
                V.tensor_tensor(pairs[:, 0:4].rearrange("p i u d -> p u i d"), src, f, ALU.mult).then_inc(qn_ready, 1)
                heads(1, 0, 8, 2, pairs[:, 4])
                heads(1, 256, 12, 4, pairs[:, 5:9, 0])
                heads(2, 0, 16, 4, pairs[:, 5:9, 1])
                heads(2, 256, 20, 2, pairs[:, 9])

            def q_columns(j, b1, b2):
                dve.wait_ge(qt_mm, 3 * j + 2)
                V.tensor_scalar(qT[j][:, 1, :, :].rearrange("p i t -> p (i t)"), bank[:, b1, :],
                                gT[:, 26:27], None, ALU.mult).then_inc(qtb_ready, 1)
                dve.wait_ge(qt_mm, 3 * j + 3)
                for g in range(2):
                    V.tensor_scalar(kT[:, g, j * P:(j + 1) * P], bank[:, b2, g * P:(g + 1) * P],
                                    gT[:, 25 + 2 * g:26 + 2 * g], None, ALU.mult).then_inc(qtb_ready, 1)

            def softmax_max(j, c):
                n = 4 * j + c
                W = (j + 1) * P
                dve.wait_ge(s_mm, n + 1)
                if n >= 2:
                    dve.wait_ge(pt_mm, n - 1 if n <= 5 else 4 + 2 * (n - 5))
                dst = S_buf[:, n % 2, 0:4 * W].rearrange("p (i w) -> p i w", i=4)
                b = bias[:, 4 * c:4 * c + 4, W - 1::-1]
                if j == 0:
                    src = bank[:, S0_BANKS[c], :].rearrange("p (i w) -> p i w", i=4)
                    link(V.tensor_tensor(dst, src, b, ALU.add))
                else:
                    for half in range(2):
                        src = bank[:, S1_BANKS[c] + half, :].rearrange("p (i w) -> p i w", i=2)
                        V.tensor_tensor(dst[:, 2 * half:2 * half + 2, :], src, b[:, 2 * half:2 * half + 2, :],
                                        ALU.add).then_inc(dve_step, 1)
                    chain[0] += 2
                    dve.wait_ge(dve_step, chain[0])
                m = slice(4 * c, 4 * c + 4)
                link(V.tensor_reduce(mx[:, j, m], dst, AX, ALU.max))
                if c < 2:
                    link(V.tensor_tensor(mx[:, j, m], mx[:, j, m], sinks[:, m], ALU.max))
                V.tensor_scalar(negm[:, j, m], mx[:, j, m], -1.0, None, ALU.mult).then_inc(m_ready, 1)
                if c < 2:
                    dve.wait_ge(m_ready, n + 1)
                    V.tensor_tensor(snk[:, j, m], sinks[:, m], negm[:, j, m], ALU.add).then_inc(snk_ready, 1)

            def attention_out(j, o_banks):
                dve.wait_ge(exp_done, 16 * (j + 1))
                dve.wait_ge(snk_exp, 2 * (j + 1))
                link(V.tensor_tensor(rsum[:, j, 0:8], rsum[:, j, 0:8], snk_e[:, j, :], ALU.add))
                link(V.reciprocal(rden[:, j, :], rsum[:, j, :]))
                dve.wait_ge(pv_mm, 4 * (j + 1))
                for g in range(2):
                    V.tensor_tensor(o_sb[j][:, g * 512:(g + 1) * 512].rearrange("p (h d) -> p h d", d=HD),
                                    bank[:, o_banks[g], :].rearrange("p (h d) -> p h d", d=HD),
                                    cols(rden[:, j, 8 * g:8 * g + 8], 8, HD), ALU.mult).then_inc(o_ready, 1)

            def groups_normed(j, nth):
                dve.wait_ge(oss_ready, 2 * (j + 1))
                r = st[:, 10 + 2 * j:12 + 2 * j]
                V.tensor_scalar(r, st[:, 30 + 2 * j:32 + 2 * j], 1.0 / 512, EPS,
                                ALU.mult, ALU.add).then_inc(stat_v, 1)
                dve.wait_ge(stat_r, nth)
                dve.wait_ge(o_ready, 2 * j + 2)
                for g in range(2):
                    o = o_sb[j][:, g * 512:(g + 1) * 512]
                    V.tensor_scalar(o, o, r[:, g:g + 1], None, ALU.mult).then_inc(on_ready, 1)

            def o_columns(j):
                for b in range(2):
                    dve.wait_ge(ot_mm, 2 * j + b + 1)
                    V.tensor_tensor(oT[j][:, 4 * b:4 * b + 4, :],
                                    bank[:, [7, 5][b], :].rearrange("p (k t) -> p k t", k=4),
                                    cols(gT[:, 16 + 4 * b:20 + 4 * b], 4, P), ALU.mult).then_inc(ot_ready, 1)

            def residual(j):
                for n in range(2):
                    dve.wait_ge(proj_mm, 2 * j + n + 1)
                    xn = xs[:, j, n * 512:(n + 1) * 512]
                    V.tensor_tensor(xn, xn, bank[:, [2, 6][n], :], ALU.add).then_inc(x1_ready, 1)

            def ffn_norm(j, nth):
                dve.wait_ge(sum_ready, 3 + j)
                V.tensor_scalar(st[:, 20 + j:21 + j], st[:, 34 + j:35 + j], 1.0 / D, EPS,
                                ALU.mult, ALU.add).then_inc(stat_v, 1)
                dve.wait_ge(stat_r, nth)
                dve.wait_ge(x1_ready, 2 * j + 2)
                dve.wait_ge(gB_ready, 2)
                V.scalar_tensor_tensor(out=h[:, j, :], in0=xs[:, j, :], scalar=st[:, 20 + j:21 + j], in1=gB[:, :],
                                       op0=ALU.mult, op1=ALU.mult).then_inc(h_ready, 1)

            head_sums(0)
            normed_heads(0)
            q_columns(0, 7, 0)
            dve.wait_ge(bias_in, 16)
            dve.wait_ge(route_in, 16 * 5)
            softmax_max(0, 0)
            head_sums(1)
            softmax_max(0, 1)
            normed_heads(1)
            softmax_max(0, 2)
            softmax_max(0, 3)
            q_columns(1, 2, 6)
            attention_out(0, (3, 4))
            groups_normed(0, 4)
            softmax_max(1, 0)
            o_columns(0)
            softmax_max(1, 1)
            residual(0)
            ffn_norm(0, 5)
            softmax_max(1, 2)
            softmax_max(1, 3)
            attention_out(1, (2, 6))
            groups_normed(1, 6)
            o_columns(1)

            keys = key.rearrange("p j r e -> p j (r e)")
            weights = weight[:, :, :, :].rearrange("p j r e -> p j (r e)")

            def select(i):
                V.tensor_tensor(
                    sel, iota[:, :].unsqueeze(1).unsqueeze(1).to_broadcast([P, NT, 2, SLOTS]),
                    keys[:, :, bass.ds(2 * i, 2)].unsqueeze(3).to_broadcast([P, NT, 2, SLOTS]),
                    ALU.is_equal).then_inc(sel_ready, 1)

            def weigh(i):
                dve.wait_ge(sel_ready, i + 1)
                V.tensor_tensor(
                    selw, sel,
                    weights[:, :, bass.ds(2 * i, 2)].unsqueeze(3).to_broadcast([P, NT, 2, SLOTS]),
                    ALU.mult).then_inc(selw_ready, 1)

            def choose(j, src, best, one_hot_out, n):
                link(V.tensor_scalar(rb[:, 0:n], src, best, None, ALU.is_equal))
                link(V.tensor_tensor(rb[:, 0:n], rb[:, 0:n], first[:, 0:n], ALU.mult))
                link(V.tensor_reduce(rs[:, j, 15:16], rb[:, 0:n], AX, ALU.max))
                link(V.tensor_scalar(one_hot_out, rb[:, 0:n], rs[:, j, 15:16], None, ALU.is_equal))

            def route(j):
                r = rs[:, j, :]
                L = lg_of(j)
                dve.wait_ge(consts, 3)
                dve.wait_ge(logit_mm, j + 1)
                link(V.tensor_tensor(L[:, :], bank[:, 3 + j, 0:G + E], r_bias[:, :], ALU.add))
                link(V.tensor_reduce(r[:, 0:1], L[:, 0:G], AX, ALU.max))
                V.tensor_scalar(r[:, 1:2], r[:, 0:1], -1.0, None, ALU.mult).then_inc(r_max, 1)
                choose(j, L[:, 0:G], r[:, 0:1], r[:, 11:11 + G], G)
                link(V.tensor_scalar(rb[:, 0:G], r[:, 11:11 + G], -1.0, -NEG, ALU.add, ALU.mult))
                link(V.tensor_tensor(em[:, :].rearrange("p (g e) -> p g e", g=G),
                                     L[:, G:].rearrange("p (g e) -> p g e", g=G),
                                     cols(r[:, 11:11 + G], G, EG), ALU.mult))
                link(V.tensor_tensor(em[:, :].rearrange("p (g e) -> p g e", g=G),
                                     em[:, :].rearrange("p (g e) -> p g e", g=G),
                                     cols(rb[:, 0:G], G, EG), ALU.add))
                link(V.tensor_reduce(r[:, 2:3], em[:, :], AX, ALU.max))
                choose(j, em[:, :], r[:, 2:3], ra[:, 0, :], E)
                link(V.scalar_tensor_tensor(out=em[:, :], in0=ra[:, 0, :], scalar=2 * NEG, in1=em[:, :],
                                            op0=ALU.mult, op1=ALU.add))
                link(V.tensor_reduce(r[:, 3:4], em[:, :], AX, ALU.max))
                V.tensor_scalar(r[:, 10:11], r[:, 2:3], -1.0, None, ALU.mult).then_inc(r_max, 1)
                choose(j, em[:, :], r[:, 3:4], ra[:, 1, :], E)
                V.tensor_tensor(member[:, j, :], ra[:, 0, :], ra[:, 1, :], ALU.add).then_inc(member_ready, 1)
                dve.wait_ge(r_exp, 2 * j + 2)
                link(V.tensor_scalar(r[:, 0:1], r[:, 9:10], 1.0, r[:, 8:9], ALU.add, ALU.mult))
                link(V.reciprocal(r[:, 1:2], r[:, 0:1]))
                link(V.tensor_tensor(r[:, 2:3], r[:, 1:2], r[:, 9:10], ALU.mult))
                link(V.tensor_scalar(rb[:, :], ra[:, 1, :], r[:, 2:3], None, ALU.mult))
                link(V.scalar_tensor_tensor(out=weight[:, j, 0, :], in0=ra[:, 0, :], scalar=r[:, 1:2], in1=rb[:, :],
                                            op0=ALU.mult, op1=ALU.add))

            route(0)
            residual(1)
            ffn_norm(1, 7)
            route(1)
            dve.wait_ge(rank_mm, 1)
            ranks = bank[:, 5, 0:2 * E].rearrange("p (j e) -> p j e", j=NT)
            link(V.scalar_tensor_tensor(out=key[:, :, 0, :], in0=ranks, scalar=1.0, in1=member[:, :, :],
                                        op0=ALU.add, op1=ALU.mult))
            link(V.tensor_scalar(key[:, :, 0, :], key[:, :, 0, :], -1.0, None, ALU.add))
            select(0)
            link(V.tensor_reduce(counts[:, 0:1], bank[:, 5, 2 * E:3 * E], AX, ALU.max))
            for r in range(1, ROUNDS_MAX):
                link(V.tensor_scalar(counts[:, r:r + 1], counts[:, 0:1], float(SLOTS * r), None, ALU.is_gt))
            link(V.tensor_reduce(rs[:, 0, 0:1], counts[:, 1:ROUNDS_MAX], AX, ALU.add))
            for c, a, b in ((1, PAIRS, PAIRS), (2, 1, 1), (3, PAIRS, PAIRS - 2), (4, 1, 0)):
                link(V.tensor_scalar(rs[:, 0, c:c + 1], rs[:, 0, 0:1], float(a), float(b), ALU.mult, ALU.add))
            V.tensor_copy(n_i[:, :], rs[:, 0, 1:5]).then_inc(n_ready, 1)
            for r in range(1, ROUNDS_MAX):
                V.tensor_copy(weight[:, :, r, :], weight[:, :, 0, :]).then_inc(key_ready, 1)
                V.tensor_scalar(key[:, :, r, :], key[:, :, 0, :], -float(SLOTS * r), None,
                                ALU.add).then_inc(key_ready, 1)
            dve.wait_ge(key_ready, 2 * (ROUNDS_MAX - 1))

            def add_mix(i, j):
                for n in range(2):
                    dve.wait_ge(mix_mm, 4 * i + (2 * j + n + 1))
                    xn = xs[:, j, n * 512:(n + 1) * 512]
                    V.tensor_tensor(xn, xn, bank[:, 4 * j + n, :], ALU.add).then_inc(mix_added, 1)

            def pair_step(previous, has_next):
                i = 0 if previous is None else previous + 1
                if previous is not None:
                    dve.wait_ge(swt_mm, previous + 1)
                weigh(i)
                if has_next:
                    dve.wait_ge(gather_mm, 2 * i + 2)
                    dve.wait_ge(selw_ready, i + 1)
                    select(i + 1)
                if previous is not None:
                    add_mix(previous, 0)
                dve.wait_ge(silu_ready, i + 1)
                dve.wait_ge(slots_read, RING * i + 8)
                V.tensor_tensor(act, silu, bank[:, 3, :], ALU.mult).then_inc(act_ready, 1)
                if previous is not None:
                    add_mix(previous, 1)
                dve.wait_ge(slots_read, RING * i + 12)
                V.tensor_copy(y_sb[:, 512:1024], bank[:, 7, :]).then_inc(y1_ready, 1)

            pair_step(None, True)
            dve.wait_ge(pp_out, 7)
            a = st[:, 40:44].rearrange("p (j n) -> p j n", j=NT)
            link(V.tensor_tensor(st[:, 44:46], a[:, :, 0], a[:, :, 1], ALU.add))
            V.tensor_scalar(st[:, 44:46], st[:, 44:46], 1.0 / D, EPS, ALU.mult, ALU.add).then_inc(pp_var, 1)
            dve.wait_ge(pp_var, 1)
            dve.wait_ge(pp_root, 1)
            link(V.reciprocal(st[:, 54:56], st[:, 46:48]))
            link(V.tensor_tensor(st[:, 56:58], st[:, 54:56], st[:, 54:56], ALU.mult))
            link(V.tensor_tensor(st[:, 56:58], st[:, 56:58], st[:, 44:46], ALU.mult))
            link(V.tensor_scalar(st[:, 56:58], st[:, 56:58], -0.5, 1.5, ALU.mult, ALU.add))
            link(V.tensor_tensor(st[:, 54:56], st[:, 54:56], st[:, 56:58], ALU.mult))
            for j in range(NT):
                V.scalar_tensor_tensor(out=PL[:, j, :], in0=PL[:, j, :], scalar=st[:, 54 + j:55 + j],
                                       in1=gB[:, :], op0=ALU.mult, op1=ALU.mult).then_inc(mix_added, 2)

            dve.wait_ge(n_ready, 1)
            before_last = dve.value_load(n_i[0:1, 2:3], min_val=PAIRS - 2, max_val=PAIRS * ROUNDS_MAX - 2)
            with dve.Fori(0, before_last) as previous:
                pair_step(previous, True)
            pair_step(before_last, False)
            add_mix(before_last + 1, 0)
            add_mix(before_last + 1, 1)

            for j in range(NT):
                dve.wait_ge(xf_mm, 2 * j + 2)
                V.tensor_copy(xfT[:, j, 4:8, :].rearrange("p k t -> p (k t)"),
                              bank[:, 3 - 2 * j, :]).then_inc(xfb_ready, 1)
                dve.wait_ge(sum_ready, 5 + j)
                V.tensor_scalar(st[:, 50 + j:51 + j], st[:, 48 + j:49 + j], 1.0 / D, EPS,
                                ALU.mult, ALU.add).then_inc(stat_v, 1)
            for j in range(NT):
                for n in range(2):
                    c = slice(n * 512, (n + 1) * 512)
                    dve.wait_ge(gate_ready, 2 * j + n + 1)
                    link(V.tensor_tensor(result[:, j, c], gate[:, j, c], PL[:, j, c], ALU.mult))
                    V.tensor_tensor(result[:, j, c], result[:, j, c], xs[:, j, c], ALU.add).then_inc(res_ready, 1)


INPUTS = ["x", "p", "rel_bias", "attn_norm", "w_in", "swa_q_norm", "swa_k_norm", "swa_sinks",
          "moba_q_norm", "moba_k_norm", "swa_out_norm", "moba_out_norm", "w_out", "ffn_norm",
          "w_router_group", "b_router_group", "w_router_expert", "b_router_expert",
          "w_exp_gate", "w_exp_up", "w_exp_down", "ple_norm", "w_ple_gate", "w_ple_proj", "ple_out_norm"]


def kernel(**inputs):
    import concourse.bacc as bacc
    from concourse.bass_utils import run_bass_kernel_spmd

    nc = bacc.Bacc("TRN2", target_bir_lowering=False, num_devices=1)
    arrays, t = {}, {}
    given = {name: np.ascontiguousarray(inputs[name]) for name in INPUTS}
    given["bucket_one_hot"] = bucket_one_hot()
    for name, a in given.items():
        arrays[f"in_{name}"] = a
        t[name] = nc.dram_tensor(f"in_{name}", a.shape, mybir.dt.from_np(a.dtype), kind="ExternalInput").ap()
    out = nc.dram_tensor("out", inputs["x"].shape, F32, kind="ExternalOutput").ap()
    build_program(nc, t, out)
    r = run_bass_kernel_spmd(nc, [arrays], core_ids=[0])
    return r.results[0]["out"]
```

```python
from contextlib import ExitStack
import math

import numpy as np
import concourse.bass as bass
from concourse import mybir

F32 = mybir.dt.float32
I32 = mybir.dt.int32
ALU = mybir.AluOpType
ACT = mybir.ActivationFunctionType
AX = mybir.AxisListType.X

P = 128
HD = 64
NEG = -1e30
EPS = 1e-6
WINDOW = 128
SLOTS = 64
BUCKETS = 32
TOEP = 384


def bucket_one_hot():
    dist = np.arange(TOEP) - 127
    n = np.maximum(dist, 0)
    exact = BUCKETS // 2
    large = exact + (np.log(np.maximum(n, 1).astype(np.float32) / exact)
                     / math.log(128 / exact) * (BUCKETS - exact)).astype(np.int32)
    bucket = np.where(n < exact, n, np.minimum(large, BUCKETS - 1))
    table = np.zeros((BUCKETS + 1, 2, TOEP), np.float32)
    for g, seen in enumerate([(dist >= 0) & (dist < WINDOW), dist >= 0]):
        table[bucket[seen], g, np.arange(TOEP)[seen]] = 1.0
        table[BUCKETS, g, ~seen] = NEG
    return table


def build_program(nc, t, out):
    x, p = t["x"][0], t["p"][0, 0]
    T, D = x.shape
    NT = T // P
    KD = D // P
    IN_W = t["w_in"].shape[2]
    NQKV = IN_W // 512
    G = t["w_router_group"].shape[2]
    E = t["w_router_expert"].shape[2]
    EG = E // G
    F = t["w_exp_gate"].shape[3]
    MF = F // P
    PD = p.shape[1]
    KP = PD // P
    PAIRS = E // 2
    RING = 12
    SLOT = 2048
    ROUNDS_MAX = T // SLOTS
    assert NT == 2 and KD == 8 and IN_W == 1536 and F == 512 and RING * SLOT == 2 * 3 * KD * F

    scratch = nc.dram_tensor("bias_scratch", (16, TOEP), F32, kind="Internal")
    ctx = ExitStack()
    with ctx:
        def sb(name, shape, dt=F32):
            return ctx.enter_context(nc.sbuf_tensor(name, shape, dt))

        def sem(name):
            return ctx.enter_context(nc.semaphore(name))

        ring = sb("ring", [P, RING, SLOT])
        w_in_sb = ring[:, RING // 2:RING, :].rearrange("p s c -> p (s c)").rearrange("p (k n) -> p k n", k=KD)
        wo_space = sb("wo_space", [P, 8192])
        w_out_sb = wo_space[:, :].rearrange("p (k n) -> p k n", k=KD)
        pg_space = sb("pg_space", [P, 8192])
        w_pg = pg_space[:, :].rearrange("p (k n) -> p k n", k=KD)
        bias = pg_space[:, 0:4096].rearrange("p (h c) -> p h c", h=16)
        S_buf = pg_space[:, 4096:6144].rearrange("p (b c) -> p b c", b=2)
        PT_buf = pg_space[:, 6144:8192].rearrange("p (b c) -> p b c", b=2)

        xo_space = sb("xo_space", [P, 2, 1024])
        xT = [xo_space[:, j, :].rearrange("p (k t) -> p k t", k=KD) for j in range(NT)]
        sq = [pg_space[:, 6144:6144 + IN_W], xo_space[:, :, :].rearrange("p j c -> p (j c)")[:, 512:512 + IN_W]]
        oT = [xo_space[:, j, :].rearrange("p (g i t) -> p g i t", g=2, i=4) for j in range(NT)]
        PL = xo_space
        qn_space = sb("qn_space", [P, 2, 1024])
        qn = qn_space[:, :, :].rearrange("p a c -> p (a c)")[:, 0:1280].rearrange("p (b c) -> p b c", b=10)
        v_head = qn_space[0:8, 0, 0:2 * TOEP].rearrange("p (g m) -> p g m", g=2)
        ple_row = qn_space[0:1, 0, :]
        hT = qn_space
        qh_space = sb("qh_space", [P, 2, 1024])
        qT = [qh_space[:, j, :].rearrange("p (g i t) -> p g i t", g=2, i=4) for j in range(NT)]
        one_hot = qh_space[0:BUCKETS + 1, 0, 0:2 * TOEP].rearrange("p (g m) -> p g m", g=2)
        o_sq = [qh_space[:, j, :].rearrange("p (g i t) -> p g i t", g=2, i=4) for j in range(NT)]
        h = qh_space
        kT_space = sb("kT_space", [P, 512])
        kT = kT_space[:, :].rearrange("p (g t) -> p g t", g=2)
        p_sb = kT_space[:, :].rearrange("p (j c) -> p j c", j=NT)
        v_space = sb("v_space", [P, 512])
        v_sb = v_space[:, :].rearrange("p (j g c) -> p j g c", j=NT, g=2)
        pT = v_space[:, :].rearrange("p (k t) -> p k t", k=KP)
        xs = sb("xs", [P, NT, D])
        gB = sb("gB", [P, D])

        xTe = wo_space[:, 4864:5888].rearrange("p (k s) -> p k s", k=KD)
        y_sb = wo_space[:, 5888:6912]
        swT = wo_space[:, 2048:2304]
        silu = wo_space[:, 2304:2816]
        act = wo_space[:, 2816:3328]
        actT = wo_space[:, 3328:3840].rearrange("p (m s) -> p m s", m=MF)
        sel = wo_space[:, 4352:4608].rearrange("p (j e s) -> p j e s", j=NT, e=2)
        selw = wo_space[:, 4608:4864].rearrange("p (j e s) -> p j e s", j=NT, e=2)
        w_pp = wo_space[:, 0:2048].rearrange("p (k n) -> p k n", k=KP)
        junk = wo_space[:, 6912:7424]
        key = wo_space[:, 7424:7680].rearrange("p (j r e) -> p j r e", j=NT, r=ROUNDS_MAX)

        xfT = ring[:, 0, :].rearrange("p (j k t) -> p j k t", j=NT, k=KD)
        gate = ring[:, 1, :].rearrange("p (j c) -> p j c", j=NT)
        result = ring[:, 2, :].rearrange("p (j c) -> p j c", j=NT)

        ident = sb("ident", [P, P])
        before = sb("before", [P, P])
        ones = sb("ones", [P, P])
        iota = sb("iota", [P, SLOTS])
        first = sb("first", [P, E])
        neghalf = sb("neghalf", [P, 24])
        gain_rows = sb("gain_rows", [36, P])
        gT = sb("gT", [P, 36])
        tbl = sb("tbl", [BUCKETS + 1, 16])
        sinks = sb("sinks", [P, 8])
        r_bias = sb("r_bias", [P, G + E])
        w_r = sb("w_r", [P, KD, G + E])
        st = sb("st", [P, 64])
        ss_h = sb("ss_h", [P, 24])
        f_h = sb("f_h", [P, 2, 24])
        mx = sb("mx", [P, 2, 16])
        negm = sb("negm", [P, 2, 16])
        rsum = sb("rsum", [P, 2, 16])
        snk = sb("snk", [P, 2, 8])
        snk_e = sb("snk_e", [P, 2, 8])
        rden = sb("rden", [P, 2, 16])
        lg = sb("lg", [P, NT, G + E])
        ra = sb("ra", [P, 2, E])
        rb = sb("rb", [P, E])
        em = sb("em", [P, E])
        rs = sb("rs", [P, 2, 16])
        member = sb("member", [P, NT, E])
        weight = sb("weight", [P, NT, ROUNDS_MAX, E])
        counts = sb("counts", [P, 4])
        n_i = sb("n_i", [P, 4], I32)

        bank = ctx.enter_context(nc.psum_tensor("bank", [P, 8, 512], F32))

        x_in = [sem(f"x_in{j}") for j in range(NT)]
        win_in = [sem(f"win_in{k}") for k in range(KD)]
        wout_in = [sem(f"wout_in{k}") for k in range(4)]
        slot_in = [sem(f"slot_in{s}") for s in range(RING)]
        wpg_in, wpp_in, p_in = sem("wpg_in"), sem("wpp_in"), sem("p_in")
        attn_in, gain_in, tbl_in, route_in = sem("attn_in"), sem("gain_in"), sem("tbl_in"), sem("route_in")
        sinks_in, ffn_in, wr_scaled = sem("sinks_in"), sem("ffn_in"), sem("wr_scaled")
        scr_out, bias_in, out_done = sem("scr_out"), sem("bias_in"), sem("out_done")
        consts, pool_chain, mask_row = sem("consts"), sem("pool_chain"), sem("mask_row")
        setup_mm, v_ready, gT_ready = sem("setup_mm"), sem("v_ready"), sem("gT_ready")
        xt_mm, xt_ready = sem("xt_mm"), sem("xt_ready")
        stat_v, stat_r, sum_ready = sem("stat_v"), sem("stat_r"), sem("sum_ready")
        qkv_mm, sq_ready, ssh_ready, qn_ready, v_copied = (sem(n) for n in (
            "qkv_mm", "sq_ready", "ssh_ready", "qn_ready", "v_copied"))
        qt_mm, qta_ready, qtb_ready = sem("qt_mm"), sem("qta_ready"), sem("qtb_ready")
        s_mm, s_added, m_ready, exp_done, snk_ready, snk_exp = (sem(n) for n in (
            "s_mm", "s_added", "m_ready", "exp_done", "snk_ready", "snk_exp"))
        pt_mm, pt_ready, pv_mm, den_ready, prob_scaled, oss_ready, oss_mm, wout_scaled = (sem(n) for n in (
            "pt_mm", "pt_ready", "pv_mm", "den_ready", "prob_scaled", "oss_ready", "oss_mm", "wout_scaled"))
        ot_ready, proj_mm, x1_ready, h_ready, ht_mm, ht_ready, logit_mm = (sem(n) for n in (
            "ot_ready", "proj_mm", "x1_ready", "h_ready", "ht_mm", "ht_ready", "logit_mm"))
        r_max, r_exp, member_ready, rank_mm, key_ready, n_ready = (sem(n) for n in (
            "r_max", "r_exp", "member_ready", "rank_mm", "key_ready", "n_ready"))
        dve_step = sem("dve_step")
        slots_read = sem("slots_read")
        sel_ready, selw_ready, gather_mm, xte_ready = (sem(n) for n in (
            "sel_ready", "selw_ready", "gather_mm", "xte_ready"))
        silu_ready, act_ready, act_mm, actt_ready, y0_ready, y1_ready = (sem(n) for n in (
            "silu_ready", "act_ready", "act_mm", "actt_ready", "y0_ready", "y1_ready"))
        swt_mm, swt_ready, mix_mm, mix_added = (sem(n) for n in ("swt_mm", "swt_ready", "mix_mm", "mix_added"))
        down_mm = sem("down_mm")
        pp_mm, pp_out, pp_var, pp_root, wpg_scaled = (sem(n) for n in ("pp_mm", "pp_out", "pp_var", "pp_root", "wpg_scaled"))
        xf_mm, xfa_ready, xfb_ready, gate_mm, gate_ready, res_ready = (sem(n) for n in (
            "xf_mm", "xfa_ready", "xfb_ready", "gate_mm", "gate_ready", "res_ready"))

        w_g, w_u, w_d = t["w_exp_gate"][0], t["w_exp_up"][0], t["w_exp_down"][0]

        def expert_slot(pair, s):
            part, half, e = s // 4, (s % 4) // 2, s % 2
            w = (w_g, w_u, w_d)[part]
            rows = w.shape[1] // 2
            v = w.rearrange("(i two) (s r) n -> i two s r n", two=2, s=2)
            v = v[bass.ds(pair, 1), e, half]
            return v.rearrange("i (k p) n -> p (i k) n", p=P)

        def slot_dst(s):
            k = 2 if s // 4 == 2 else 4
            return ring[:, s, :].rearrange("p (k n) -> p k n", k=k)

        def by_group(a):
            return a.rearrange("p (g h) -> p g h", g=2)

        def lg_of(j):
            return lg[:, j, :]

        XT_BANKS = [(6, 7), (4, 5)]
        S0_BANKS = [1, 2, 6, 0]
        S1_BANKS = [(0, 6), (3, 4), (3, 4), (3, 4)]
        P_BANKS = (7, 5)
        O_BANKS = (1, 2)
        PJ_BANKS = [((1, 2), (0, 6)), ((1, 0), (2, 6))]
        PLE_BANKS = (6, 3)
        GATE = [(0, 0, 512, 6), (0, 512, 512, 7), (1, 0, 512, 4), (1, 512, 256, 5), (1, 768, 256, 0)]
        H_BANKS = (0, 6)

        block = ctx.enter_context(nc.Block())

        @block.sync
        def _(sp):
            for j in range(NT):
                sp.dma_start(xs[:, j, :], x[j * P:(j + 1) * P, :]).then_inc(x_in[j], 16)
            for k in range(KD):
                sp.dma_start(w_in_sb[:, k, :], t["w_in"][0, k * P:(k + 1) * P, :]).then_inc(win_in[k], 16)
            wo = t["w_out"][0].rearrange("(g u i d) n -> g u d i n", g=2, u=2, i=4)
            sp.wait_ge(v_ready, 2)
            sp.dma_start(scratch.ap().rearrange("(g h) m -> h g m", g=2), v_head).then_inc(scr_out, 16)
            for q in range(4):
                if q == 2:
                    sp.wait_ge(scr_out, 16)
                    toeplitz = bass.AP(scratch, 0, [[1, P], [TOEP, 16], [1, 2 * P]])
                    sp.dma_start(bias, toeplitz).then_inc(bias_in, 16)
                g, u = q // 2, q % 2
                sp.dma_start(w_out_sb[u * HD:(u + 1) * HD, 4 * g:4 * g + 4, :], wo[g, u]).then_inc(wout_in[q], 16)
            for s in range(RING // 2):
                sp.dma_start(slot_dst(s), expert_slot(0, s)).then_inc(slot_in[s], 16)
            sp.dma_start(gB[:, :], t["ffn_norm"].partition_broadcast(P).rearrange("q a c -> q (a c)")).then_inc(ffn_in, 16)
            sp.wait_ge(qkv_mm, 2)
            for s in range(RING // 2, RING):
                sp.dma_start(slot_dst(s), expert_slot(0, s)).then_inc(slot_in[s], 16)
            sp.wait_ge(s_mm, 8)
            sp.dma_start(p_sb, p.rearrange("(j p) c -> p j c", p=P)).then_inc(p_in, 16)
            sp.wait_ge(proj_mm, 6)
            sp.dma_start(w_pp, t["w_ple_proj"][0].rearrange("(k p) n -> p k n", p=P)).then_inc(wpp_in, 16)
            sp.wait_ge(logit_mm, 1)
            sp.dma_start(ple_row, t["ple_out_norm"]).then_inc(p_in, 16)
            sp.wait_ge(pv_mm, 4)
            sp.dma_start(w_pg, t["w_ple_gate"][0].rearrange("(k p) n -> p k n", p=P)).then_inc(wpg_in, 16)

            def pair_loads(previous, pair):
                for s in range(RING):
                    sp.wait_ge(slots_read, RING * previous + (s + 1))
                    sp.dma_start(slot_dst(s), expert_slot(pair, s)).then_inc(slot_in[s], 16)

            with sp.Fori(0, PAIRS - 1) as previous:
                pair_loads(previous, previous + 1)
            sp.wait_ge(n_ready, 1)
            more = sp.value_load(n_i[0:1, 3:4], min_val=0, max_val=ROUNDS_MAX - 1)
            with sp.If(more > 0):
                with sp.Fori(0, more) as r:
                    with sp.Fori(0, PAIRS) as pair:
                        pair_loads(r * PAIRS + pair + (PAIRS - 1), pair)
            for n, (j, c0, width, b) in enumerate(GATE):
                sp.wait_ge(res_ready, n + 1)
                sp.dma_start(out[0, j * P:(j + 1) * P, c0:c0 + width],
                             result[:, j, c0:c0 + width]).then_inc(out_done, 16)
            sp.wait_ge(out_done, 16 * len(GATE))

        @block.gpsimd
        def _(pool):
            chain = [0]

            def link(ins):
                chain[0] += 1
                ins.then_inc(pool_chain, 1)
                pool.wait_ge(pool_chain, chain[0])

            link(pool.memset(ident[:, :], 0.0))
            link(pool.affine_select(out=ident[:, :], in_=ident[:, :], compare_op=ALU.not_equal, fill=1.0,
                                    base=0, pattern=[[-1, P]], channel_multiplier=1))
            link(pool.memset(ones[:, :], 1.0))
            pool.affine_select(out=before[:, :], in_=ones[:, :], compare_op=ALU.is_gt, fill=0.0,
                               base=0, pattern=[[1, P]], channel_multiplier=-1).then_inc(consts, 1)
            pool.iota(iota[:, :], [[1, SLOTS]], base=1, channel_multiplier=0,
                      allow_small_or_imprecise_dtypes=True).then_inc(consts, 1)
            pool.iota(first[:, :], [[-1, E]], base=E, channel_multiplier=0,
                      allow_small_or_imprecise_dtypes=True).then_inc(consts, 1)
            link(pool.memset(neghalf[:, :], -0.5))

            def rsqrt(n, dst, src):
                pool.wait_ge(stat_v, n)
                pool.tensor_tensor(dst, src, neghalf[:, 0:dst.shape[1]], ALU.pow).then_inc(stat_r, 1)

            def rsqrt_heads(n, j, h0, h1):
                pool.wait_ge(stat_v, n)
                pool.tensor_tensor(by_group(f_h[:, j, :])[:, :, h0:h1], by_group(ss_h[:, :])[:, :, h0:h1],
                                   by_group(neghalf[:, :])[:, :, h0:h1], ALU.pow).then_inc(stat_r, 1)

            def ffn_norm(j):
                pool.wait_ge(ffn_in, 16)
                pool.wait_ge(x1_ready, 4 * j + 4)
                pool.wait_ge(stat_r, 7 + 2 * j)
                link(pool.tensor_scalar(h[:, j, :], xs[:, j, :], st[:, 20 + j:21 + j], 1.0, ALU.mult, ALU.mult))
                pool.tensor_tensor(h[:, j, :], h[:, j, :], gB[:, :], ALU.mult).then_inc(h_ready, 1)

            rsqrt(1, st[:, 2:4], st[:, 2:4])
            rsqrt_heads(2, 0, 8, 10)
            rsqrt_heads(3, 0, 0, 8)

            pool.wait_ge(gT_ready, 2)
            for k in range(KD):
                for u in range(2):
                    pool.wait_ge(wout_in[2 * (k // 4) + u], 16)
                pool.tensor_scalar(w_out_sb[:, k, :], w_out_sb[:, k, :], gT[:, 16 + k:17 + k], 1.0,
                                   ALU.mult, ALU.mult).then_inc(wout_scaled, 1)

            def probs_scaled(j, c):
                n = 4 * j + c
                W = (j + 1) * P
                pool.wait_ge(exp_done, 4 * n + 4)
                pool.wait_ge(den_ready, n + 1)
                s = S_buf[:, n % 2, 0:4 * W].rearrange("p (i w) -> p i w", i=4)
                d = rden[:, j, 4 * c:4 * c + 4].unsqueeze(2).to_broadcast([P, 4, W])
                pool.tensor_tensor(s, s, d, ALU.mult).then_inc(prob_scaled, 1)

            probs_scaled(0, 0)
            probs_scaled(0, 1)
            probs_scaled(0, 2)
            probs_scaled(0, 3)
            rsqrt_heads(4, 1, 8, 10)
            rsqrt_heads(5, 1, 0, 8)
            probs_scaled(1, 0)
            rsqrt(6, st[:, 10:12], st[:, 10:12])
            probs_scaled(1, 1)
            probs_scaled(1, 2)
            probs_scaled(1, 3)
            rsqrt(7, st[:, 20:21], st[:, 20:21])
            ffn_norm(0)
            rsqrt(8, st[:, 12:14], st[:, 12:14])
            rsqrt(9, st[:, 21:22], st[:, 21:22])
            ffn_norm(1)

            pool.wait_ge(wpg_in, 16)
            for k in range(KD):
                pool.tensor_scalar(w_pg[:, k, :], w_pg[:, k, :], gT[:, 8 + k:9 + k], 1.0,
                                   ALU.mult, ALU.mult).then_inc(wpg_scaled, 1)
            rsqrt(10, st[:, 52:53], st[:, 50:51])
            rsqrt(11, st[:, 53:54], st[:, 51:52])

        @block.tensor
        def _(pe):
            pe.wait_ge(consts, 3)
            pe.wait_ge(pool_chain, 3)
            pe.wait_ge(attn_in, 16)
            pe.transpose(bank[:, 7, 0:8], gain_rows[0:8, :], ident[0:8, 0:8]).then_inc(setup_mm, 1)
            pe.wait_ge(gT_ready, 1)
            for j in range(NT):
                pe.wait_ge(x_in[j], 16)
                for b in range(2):
                    for k in range(4):
                        mm = pe.transpose(bank[:, XT_BANKS[j][b], k * P:(k + 1) * P],
                                          xs[:, j, (4 * b + k) * P:(4 * b + k + 1) * P], ident[:, :])
                    mm.then_inc(xt_mm, 1)

            def qkv(j, chunks):
                for k in chunks:
                    if j == 0:
                        pe.wait_ge(win_in[k], 16)
                    for n in range(NQKV):
                        mm = pe.matmul(bank[:, 3 * j + n, :], xT[j][:, k, :], w_in_sb[:, k, n * 512:(n + 1) * 512],
                                       start=(k == 0), stop=(k == KD - 1))
                    if k == KD - 1:
                        mm.then_inc(qkv_mm, 1)

            def bias_by_distance():
                pe.wait_ge(tbl_in, 32)
                pe.wait_ge(mask_row, 1)
                for g in range(2):
                    pe.matmul(bank[0:8, 6 + g, 0:TOEP], tbl[:, 8 * g:8 * g + 8], one_hot[:, g, :],
                              start=True, stop=True).then_inc(setup_mm, 1)

            def other_gains():
                pe.wait_ge(gain_in, 16 * 8)
                pe.wait_ge(v_ready, 2)
                pe.transpose(bank[:, 7, 0:36], gain_rows[:, :], ident[0:36, 0:36]).then_inc(setup_mm, 1)

            def transposes(b, blocks):
                for n, blk in enumerate(blocks):
                    mm = pe.transpose(bank[:, b, n * P:(n + 1) * P], qn[:, blk, :], ident[:, :])
                mm.then_inc(qt_mm, 1)

            def q_transposes(j, b0, b1):
                pe.wait_ge(qn_ready, 5 * j + 1)
                transposes(b0, [0, 1, 2, 3])
                pe.wait_ge(qn_ready, 5 * j + 3)
                transposes(b1, [5, 6, 7, 8])

            def k_transposes(j, b):
                pe.wait_ge(qn_ready, 5 * j + 5)
                pe.wait_ge(v_copied, 2 * j + 2)
                transposes(b, [4, 9])

            def scores(j, c):
                g, u = c // 2, c % 2
                rows = slice(u * HD, (u + 1) * HD)
                W = (j + 1) * P
                for i in range(4):
                    if j == 0:
                        dst = bank[:, S0_BANKS[c], i * P:(i + 1) * P]
                    else:
                        dst = bank[:, S1_BANKS[c][i // 2], (i % 2) * W:(i % 2 + 1) * W]
                    mm = pe.matmul(dst, qT[j][rows, g, i, :], kT[rows, g, 0:W], start=True, stop=True)
                mm.then_inc(s_mm, 1)

            def prob_transposes(j, c):
                n = 4 * j + c
                W = (j + 1) * P
                pe.wait_ge(prob_scaled, n + 1)
                if n:
                    pe.wait_ge(pt_ready, c if j == 0 else 4 + 2 * c)
                src = S_buf[:, n % 2, 0:4 * W].rearrange("p (i w) -> p i w", i=4)
                for kb in range(j + 1):
                    for i in range(4):
                        mm = pe.transpose(bank[:, P_BANKS[kb], i * P:(i + 1) * P],
                                          src[:, i, kb * P:(kb + 1) * P], ident[:, :])
                    mm.then_inc(pt_mm, 1)

            def probs_v(j, g):
                pe.wait_ge(pt_ready, 2 * g + 2 if j == 0 else 4 + 4 * g + 4)
                if j:
                    pe.wait_ge(x1_ready, g + 1)
                for kb in range(j + 1):
                    for u in range(2):
                        mm = pe.matmul(bank[u * HD:(u + 1) * HD, O_BANKS[g], :],
                                       v_sb[:, kb, g, u * HD:(u + 1) * HD], PT_buf[:, u, kb * 512:(kb + 1) * 512],
                                       start=(kb == 0), stop=(kb == j))
                mm.then_inc(pv_mm, 1)

            def o_sums(j):
                pe.wait_ge(oss_ready, 2 * j + 2)
                for g in range(2):
                    for i in range(4):
                        mm = pe.matmul(bank[:, 7, g:g + 1], o_sq[j][:, g, i, :], ones[:, 0:1],
                                       start=(i == 0), stop=(i == 3))
                mm.then_inc(oss_mm, 1)

            def out_projection(j, g, n):
                pe.wait_ge(ot_ready, 2 * j + g + 1)
                pe.wait_ge(wout_scaled, 4 * g + 4)
                for i in range(4):
                    mm = pe.matmul(bank[:, PJ_BANKS[j][g][n], :], oT[j][:, g, i, :],
                                   w_out_sb[:, 4 * g + i, n * 512:(n + 1) * 512], start=(i == 0), stop=(i == 3))
                mm.then_inc(proj_mm, 1)

            def logits(j, product):
                if not product:
                    for b in range(2):
                        pe.wait_ge(x1_ready, 4 * j + 2 + b + 1)
                        if j:
                            pe.wait_ge(ht_ready, b + 1)
                        for k in range(4):
                            mm = pe.transpose(bank[:, H_BANKS[b], k * P:(k + 1) * P],
                                              xs[:, j, (4 * b + k) * P:(4 * b + k + 1) * P], ident[:, :])
                        mm.then_inc(ht_mm, 1)
                    return
                pe.wait_ge(wr_scaled, 1)
                pe.wait_ge(m_ready, 8)
                for k in range(KD):
                    if k % 4 == 0:
                        pe.wait_ge(ht_ready, 2 * j + k // 4 + 1)
                    mm = pe.matmul(bank[:, 3 + j, 0:G + E], hT[:, j, k * P:(k + 1) * P], w_r[:, k, :],
                                   start=(k == 0), stop=(k == KD - 1))
                mm.then_inc(logit_mm, 1)

            pe.wait_ge(xt_ready, 2)
            qkv(0, range(3))
            bias_by_distance()
            qkv(0, range(3, KD))
            other_gains()
            pe.wait_ge(xt_ready, 4)
            qkv(1, range(2))
            pe.wait_ge(gT_ready, 2)
            q_transposes(0, 6, 7)
            k_transposes(0, 0)
            qkv(1, range(2, 3))
            pe.wait_ge(qta_ready, 1)
            pe.wait_ge(qtb_ready, 3)
            for c in range(4):
                scores(0, c)
            qkv(1, range(3, 5))
            prob_transposes(0, 0)
            qkv(1, range(5, 6))
            prob_transposes(0, 1)
            probs_v(0, 0)
            qkv(1, range(6, 7))
            prob_transposes(0, 2)
            qkv(1, range(7, KD))
            prob_transposes(0, 3)
            out_projection(0, 0, 0)
            pe.wait_ge(m_ready, 4)
            q_transposes(1, 3, 6)
            probs_v(0, 1)
            k_transposes(1, 5)
            pe.wait_ge(qta_ready, 2)
            pe.wait_ge(qtb_ready, 6)
            scores(1, 0)
            scores(1, 1)
            o_sums(0)
            pe.wait_ge(ot_ready, 2)
            out_projection(0, 0, 1)
            pe.wait_ge(m_ready, 5)
            out_projection(0, 1, 0)
            pe.wait_ge(stat_v, 6)
            prob_transposes(1, 0)
            pe.wait_ge(m_ready, 6)
            scores(1, 2)
            prob_transposes(1, 1)
            out_projection(0, 1, 1)
            pe.wait_ge(m_ready, 7)
            scores(1, 3)
            probs_v(1, 0)
            prob_transposes(1, 2)
            logits(0, False)
            out_projection(1, 0, 0)
            prob_transposes(1, 3)
            logits(0, True)
            out_projection(1, 0, 1)
            probs_v(1, 1)
            out_projection(1, 1, 0)
            o_sums(1)
            out_projection(1, 1, 1)

            def project_p(j, n):
                for k in range(KP):
                    mm = pe.matmul(bank[:, 5 - n, :], pT[:, k, j * P:(j + 1) * P],
                                   w_pp[:, k, n * 512:(n + 1) * 512], start=(k == 0), stop=(k == KP - 1))
                mm.then_inc(pp_mm, 1)

            pe.wait_ge(member_ready, 1)
            pe.wait_ge(stat_v, 8)
            pe.matmul(bank[:, 7, 0:E], before[:, :], member[:, 0, :], start=True, stop=True)
            pe.matmul(bank[:, 7, E:2 * E], ones[:, :], member[:, 0, :], start=True, stop=False)
            logits(1, False)
            logits(1, True)
            pe.wait_ge(p_in, 32)
            for k in range(KP):
                for j in range(NT):
                    mm = pe.transpose(bank[:, 5, (2 * k + j) * P:(2 * k + j + 1) * P],
                                      p_sb[:, j, k * P:(k + 1) * P], ident[:, :])
            mm.then_inc(pp_mm, 1)
            for n in range(2):
                pe.matmul(bank[:, PLE_BANKS[n], :], ones[0:1, :], ple_row[:, n * 512:(n + 1) * 512],
                          start=True, stop=True).then_inc(pp_mm, 1)
            pe.wait_ge(wpp_in, 16)
            pe.wait_ge(pp_out, 1)
            project_p(0, 0)
            pe.wait_ge(member_ready, 2)
            pe.matmul(bank[:, 7, E:2 * E], before[:, :], member[:, 1, :], start=False, stop=True).then_inc(rank_mm, 1)
            for j in range(NT):
                mm = pe.matmul(bank[:, 4, 0:E], ones[:, :], member[:, j, :], start=(j == 0), stop=(j == NT - 1))
            mm.then_inc(rank_mm, 1)

            def gather(i, b):
                if b == 0:
                    pe.wait_ge(sel_ready, i + 1)
                    pe.wait_ge(h_ready, 2)
                for k in range(4 * b, 4 * b + 4):
                    for j in range(NT):
                        mm = pe.matmul(bank[:, b, (k % 4) * P:(k % 4 + 1) * P], h[:, j, k * P:(k + 1) * P],
                                       sel[:, j, :, :].rearrange("p e s -> p (e s)"),
                                       start=(j == 0), stop=(j == NT - 1))
                mm.then_inc(gather_mm, 1)

            def weights(i, part, half, e):
                s = 4 * part + 2 * half + e
                pe.wait_ge(slot_in[s], 16 * i + 16)
                return ring[:, s, :].rearrange("p (k n) -> p k n", k=2 if part == 2 else 4)

            def gate_or_up(i, part):
                for half in range(2):
                    if part == 0:
                        pe.wait_ge(xte_ready, 2 * i + (half + 1))
                    w = [weights(i, part, half, e) for e in range(2)]
                    for k in range(4):
                        for e in range(2):
                            mm = pe.matmul(bank[e * SLOTS:(e + 1) * SLOTS, 2 + part, :],
                                           xTe[:, 4 * half + k, e * SLOTS:(e + 1) * SLOTS], w[e][:, k, :],
                                           start=(half == 0 and k == 0), stop=(half == 1 and k == 3))
                            if k == 3:
                                mm.then_inc(slots_read, 1)

            def down(i):
                pe.wait_ge(actt_ready, i + 1)
                for half in range(2):
                    w = [weights(i, 2, half, e) for e in range(2)]
                    for n in range(2):
                        for m in range(2):
                            for e in range(2):
                                mm = pe.matmul(bank[e * SLOTS:(e + 1) * SLOTS, 6 + n, :],
                                               actT[:, 2 * half + m, e * SLOTS:(e + 1) * SLOTS],
                                               w[e][:, m, n * 512:(n + 1) * 512],
                                               start=(half == 0 and m == 0), stop=(half == 1 and m == 1))
                                if n == 1 and m == 1:
                                    mm.then_inc(slots_read, 1)
                        if half == 1 and n == 0:
                            mm.then_inc(down_mm, 1)

            def act_transposes(i):
                pe.wait_ge(act_ready, i + 1)
                for m in range(MF):
                    mm = pe.transpose(bank[:, 4, m * P:(m + 1) * P], act[:, m * P:(m + 1) * P], ident[:, :])
                mm.then_inc(act_mm, 1)

            def weight_transposes(i):
                pe.wait_ge(selw_ready, i + 1)
                for j in range(NT):
                    mm = pe.transpose(bank[:, 5, j * P:(j + 1) * P],
                                      selw[:, j, :, :].rearrange("p e s -> p (e s)"), ident[:, :])
                mm.then_inc(swt_mm, 1)

            def mix(i, j):
                if j == 0:
                    pe.wait_ge(swt_ready, i + 1)
                for n in range(2):
                    if j == 0:
                        pe.wait_ge((y0_ready, y1_ready)[n], i + 1)
                    pe.matmul(bank[:, 4 * j + n, :], swT[:, j * P:(j + 1) * P], y_sb[:, n * 512:(n + 1) * 512],
                              start=True, stop=True).then_inc(mix_mm, 1)

            def pair_step(previous, has_next):
                i = 0 if previous is None else previous + 1
                if previous is not None:
                    pe.wait_ge(act_ready, previous + 1)
                gate_or_up(i, 0)
                if previous is not None:
                    mix(previous, 0)
                gate_or_up(i, 1)
                if previous is not None:
                    pe.wait_ge(mix_added, 4 * previous + 4)
                    mix(previous, 1)
                    pe.wait_ge(mix_added, 4 * previous + 6)
                if has_next:
                    gather(i + 1, 0)
                if previous is not None:
                    pe.wait_ge(mix_added, 4 * previous + 7)
                act_transposes(i)
                if has_next:
                    gather(i + 1, 1)
                if previous is not None:
                    pe.wait_ge(mix_added, 4 * previous + 8)
                weight_transposes(i)
                if previous is not None:
                    pe.wait_ge(y0_ready, previous + 1)
                    pe.wait_ge(y1_ready, previous + 1)
                down(i)

            gather(0, 0)
            gather(0, 1)
            pe.wait_ge(pp_out, 4)
            pair_step(None, True)
            pe.wait_ge(swt_ready, 1)
            for j, n in ((0, 1), (1, 0), (1, 1)):
                pe.wait_ge(pp_out, 2 + 2 * j + n)
                project_p(j, n)
            before_last = pe.value_load(n_i[0:1, 2:3], min_val=PAIRS - 2, max_val=PAIRS * ROUNDS_MAX - 2)
            n_pairs = pe.value_load(n_i[0:1, 0:1], min_val=PAIRS, max_val=PAIRS * ROUNDS_MAX)
            with pe.Fori(0, before_last) as previous:
                pair_step(previous, True)
            pair_step(before_last, False)
            for j in range(NT):
                mix(before_last + 1, j)

            for j in range(NT):
                pe.wait_ge(mix_added, 4 * n_pairs + 2 * (j + 1))
                for b in range(2):
                    for k in range(4):
                        mm = pe.transpose(bank[:, 2 - 2 * j + b, k * P:(k + 1) * P],
                                          xs[:, j, (4 * b + k) * P:(4 * b + k + 1) * P], ident[:, :])
                    mm.then_inc(xf_mm, 1)
            pe.wait_ge(wpg_scaled, KD)
            for j, c0, width, b in GATE:
                pe.wait_ge(xfa_ready, j + 1)
                pe.wait_ge(xfb_ready, j + 1)
                for k in range(KD):
                    mm = pe.matmul(bank[:, b, 0:width], xfT[:, j, k, :], w_pg[:, k, c0:c0 + width],
                                   start=(k == 0), stop=(k == KD - 1))
                mm.then_inc(gate_mm, 1)

        @block.scalar
        def _(actv):
            ACTF = nc.scalar.activation

            def small(dst, src, s):
                actv.dma_start(dst, src).then_inc(s, 16)

            rows = lambda a: a.rearrange("(r c) -> r c", c=P)
            row = lambda name: t[name].partition_broadcast(P).rearrange("q a c -> q (a c)")
            small(gain_rows[0:8, :], rows(t["attn_norm"][0]), attn_in)
            small(tbl[0:BUCKETS, :], t["rel_bias"], tbl_in)
            small(one_hot, t["bucket_one_hot"], tbl_in)
            for n, name in enumerate(["swa_q_norm", "swa_k_norm", "moba_q_norm", "moba_k_norm"]):
                small(gain_rows[24 + n:25 + n, :].rearrange("a (u d) -> a u d", u=2),
                      t[name].partition_broadcast(2).rearrange("u a d -> a u d"), gain_in)
            for g, name in enumerate(["swa_out_norm", "moba_out_norm"]):
                small(gain_rows[16 + 4 * g:20 + 4 * g, :].rearrange("i (u d) -> i u d", u=2),
                      t[name][0].rearrange("(u i d) -> i u d", u=2, i=4), gain_in)
            small(gain_rows[8:16, :], rows(t["ple_norm"][0]), gain_in)
            small(gain_rows[28:36, :], rows(t["ffn_norm"][0]), gain_in)
            small(sinks[:, :], row("swa_sinks"), sinks_in)
            small(w_r[:, :, 0:G], t["w_router_group"][0].rearrange("(k p) g -> p k g", p=P), route_in)
            small(w_r[:, :, G:G + E], t["w_router_expert"][0].rearrange("(k p) g -> p k g", p=P), route_in)
            small(r_bias[:, 0:G], row("b_router_group"), route_in)
            small(r_bias[:, G:G + E], row("b_router_expert"), route_in)

            for j in range(NT):
                actv.wait_ge(x_in[j], 16)
                ACTF(sq[0][:, 0:D], xs[:, j, :], ACT.Square, accum_out=st[:, j:j + 1]).then_inc(sum_ready, 1)
                actv.wait_ge(sum_ready, j + 1)

            actv.wait_ge(setup_mm, 3)
            for g in range(2):
                actv.copy(v_head[:, g, :], bank[0:8, 6 + g, 0:TOEP]).then_inc(v_ready, 1)

            def squares(j):
                actv.wait_ge(qkv_mm, j + 1)
                actv.wait_ge(stat_r, 1)
                for n in range(NQKV):
                    ACTF(sq[j][:, n * 512:(n + 1) * 512], bank[:, 3 * j + n, :], ACT.Square,
                         scale=st[:, 2 + j:3 + j]).then_inc(sq_ready, 1)
                    if n:
                        at = (128, 384)[n - 1]
                        actv.mul(v_sb[:, j, n - 1, :], bank[:, 3 * j + n, at:at + P],
                                 st[:, 2 + j:3 + j]).then_inc(v_copied, 1)

            def q_columns(j, b0):
                actv.wait_ge(gT_ready, 4)
                actv.wait_ge(qt_mm, 3 * j + 1)
                actv.mul(qT[j][:, 0, :, :].rearrange("p i t -> p (i t)"), bank[:, b0, :],
                         gT[:, 24:25]).then_inc(qta_ready, 1)

            def exps(j, c):
                n = 4 * j + c
                W = (j + 1) * P
                actv.wait_ge(m_ready, n + 1)
                for i in range(4):
                    hh = 4 * c + i
                    s = S_buf[:, n % 2, i * W:(i + 1) * W]
                    ACTF(s, s, ACT.Exp, bias=negm[:, j, hh:hh + 1], accum_out=rsum[:, j, hh:hh + 1]).then_inc(exp_done, 1)
                if c < 2:
                    actv.wait_ge(snk_ready, 2 * j + c + 1)
                    ACTF(snk_e[:, j, 4 * c:4 * c + 4], snk[:, j, 4 * c:4 * c + 4], ACT.Exp).then_inc(snk_exp, 1)

            def prob_columns(j, c):
                n = 4 * j + c
                for b in range(j + 1):
                    done = c + 1 if j == 0 else 4 + 2 * c + b + 1
                    actv.wait_ge(pt_mm, done)
                    if n == 0:
                        actv.wait_ge(ssh_ready, 1)
                    actv.copy(PT_buf[:, n % 2, b * 512:(b + 1) * 512], bank[:, P_BANKS[b], :]).then_inc(pt_ready, 1)

            def o_columns(j, g):
                actv.wait_ge(pv_mm, 2 * j + g + 1)
                if j == 0 and g == 1:
                    actv.wait_ge(ssh_ready, 2)
                actv.copy(oT[j][:, g, :, :].rearrange("p i t -> p (i t)"), bank[:, O_BANKS[g], :]).then_inc(ot_ready, 1)
                actv.wait_ge(ot_ready, 2 * j + g + 1)
                ACTF(o_sq[j][:, g, :, :], oT[j][:, g, :, :], ACT.Square).then_inc(oss_ready, 1)

            def x_squares(j):
                actv.wait_ge(x1_ready, 4 * j + 4)
                actv.wait_ge(oss_mm, j + 1)
                ACTF(qh_space[:, j, :], xs[:, j, :], ACT.Square, accum_out=st[:, 34 + j:35 + j]).then_inc(sum_ready, 1)

            def h_columns(j, b):
                actv.wait_ge(ht_mm, 2 * j + b + 1)
                actv.copy(hT[:, j, b * 512:(b + 1) * 512], bank[:, H_BANKS[b], :]).then_inc(ht_ready, 1)

            squares(0)
            q_columns(0, 6)
            exps(0, 0)
            exps(0, 1)
            prob_columns(0, 0)
            exps(0, 2)
            prob_columns(0, 1)
            exps(0, 3)
            o_columns(0, 0)
            prob_columns(0, 2)
            squares(1)
            prob_columns(0, 3)
            q_columns(1, 3)
            o_columns(0, 1)
            exps(1, 0)
            exps(1, 1)
            prob_columns(1, 0)
            prob_columns(1, 1)
            exps(1, 2)
            o_columns(1, 0)
            prob_columns(1, 2)
            exps(1, 3)
            x_squares(0)
            h_columns(0, 0)
            h_columns(0, 1)
            prob_columns(1, 3)
            o_columns(1, 1)

            def group_exps(j):
                actv.wait_ge(r_max, 2 * j + 1)
                ACTF(rs[:, j, 4:8], lg_of(j)[:, 0:G], ACT.Exp, bias=rs[:, j, 1:2],
                     accum_out=rs[:, j, 8:9]).then_inc(r_exp, 1)

            def expert_exp(j):
                actv.wait_ge(r_max, 2 * j + 2)
                ACTF(rs[:, j, 9:10], rs[:, j, 3:4], ACT.Exp, bias=rs[:, j, 10:11]).then_inc(r_exp, 1)

            group_exps(0)
            expert_exp(0)
            h_columns(1, 0)
            x_squares(1)
            h_columns(1, 1)
            group_exps(1)
            actv.wait_ge(pp_mm, 1)
            actv.copy(pT.rearrange("p k t -> p (k t)"), bank[:, 5, :]).then_inc(pp_out, 1)
            expert_exp(1)

            def tokens_in(i, b):
                actv.wait_ge(gather_mm, 2 * i + (b + 1))
                actv.copy(xTe[:, 4 * b:4 * b + 4, :].rearrange("p k s -> p (k s)"),
                          bank[:, b, :]).then_inc(xte_ready, 1)

            def pair_step(previous, has_next):
                i = 0 if previous is None else previous + 1
                actv.wait_ge(slots_read, RING * i + 4)
                if previous is not None:
                    actv.wait_ge(act_ready, previous + 1)
                ACTF(silu, bank[:, 2, :], ACT.Silu).then_inc(silu_ready, 1)
                if has_next:
                    tokens_in(i + 1, 0)
                actv.wait_ge(act_mm, i + 1)
                actv.copy(actT.rearrange("p m s -> p (m s)"), bank[:, 4, :]).then_inc(actt_ready, 1)
                if has_next:
                    tokens_in(i + 1, 1)
                actv.wait_ge(swt_mm, i + 1)
                actv.copy(swT, bank[:, 5, 0:NT * P]).then_inc(swt_ready, 1)
                actv.wait_ge(down_mm, i + 1)
                actv.copy(y_sb[:, 0:512], bank[:, 6, :]).then_inc(y0_ready, 1)

            def projected_p(j, n):
                actv.wait_ge(pp_mm, 4 + 2 * j + n)
                actv.copy(PL[:, j, n * 512:(n + 1) * 512], bank[:, 5 - n, :])
                actv.wait_ge(pp_out, 3 + 2 * j + n)
                ACTF(junk, bank[:, 5 - n, :], ACT.Square,
                     accum_out=st[:, 40 + 2 * j + n:41 + 2 * j + n]).then_inc(pp_out, 1)

            actv.wait_ge(h_ready, 2)
            for n in range(2):
                actv.wait_ge(pp_mm, 2 + n)
                actv.copy(gB[:, n * 512:(n + 1) * 512], bank[:, PLE_BANKS[n], :]).then_inc(pp_out, 1)
            projected_p(0, 0)
            tokens_in(0, 0)
            tokens_in(0, 1)
            pair_step(None, True)
            for j, n in ((0, 1), (1, 0), (1, 1)):
                projected_p(j, n)
            actv.wait_ge(pp_var, 1)
            ACTF(st[:, 46:48], st[:, 44:46], ACT.Sqrt).then_inc(pp_root, 1)

            actv.wait_ge(n_ready, 1)
            n_pairs = actv.value_load(n_i[0:1, 0:1], min_val=PAIRS, max_val=PAIRS * ROUNDS_MAX)
            before_last = actv.value_load(n_i[0:1, 2:3], min_val=PAIRS - 2, max_val=PAIRS * ROUNDS_MAX - 2)
            with actv.Fori(0, before_last) as previous:
                pair_step(previous, True)
            pair_step(before_last, False)

            for j in range(NT):
                actv.wait_ge(xf_mm, 2 * j + 1)
                actv.copy(xfT[:, j, 0:4, :].rearrange("p k t -> p (k t)"), bank[:, 2 - 2 * j, :]).then_inc(xfa_ready, 1)
                actv.wait_ge(mix_added, 4 * n_pairs + 2 * (j + 1))
                ACTF(ring[:, 3 + j, 0:D], xs[:, j, :], ACT.Square, accum_out=st[:, 48 + j:49 + j]).then_inc(sum_ready, 1)
            for n, (j, c0, width, b) in enumerate(GATE):
                actv.wait_ge(stat_r, 10 + j)
                actv.wait_ge(gate_mm, n + 1)
                ACTF(gate[:, j, c0:c0 + width], bank[:, b, 0:width], ACT.Sigmoid,
                     scale=st[:, 52 + j:53 + j]).then_inc(gate_ready, 1)

        @block.vector
        def _(dve):
            chain = [0]

            def link(ins):
                chain[0] += 1
                ins.then_inc(dve_step, 1)
                dve.wait_ge(dve_step, chain[0])

            V = nc.vector

            def cols(a, n, w):
                return a.unsqueeze(2).to_broadcast([P, n, w])

            V.memset(tbl[BUCKETS:BUCKETS + 1, :], 1.0).then_inc(mask_row, 1)
            dve.wait_ge(setup_mm, 1)
            V.tensor_copy(gT[:, 0:8], bank[:, 7, 0:8]).then_inc(gT_ready, 1)
            dve.wait_ge(gT_ready, 1)
            for j in range(NT):
                for b in range(2):
                    dve.wait_ge(xt_mm, 2 * j + b + 1)
                    V.tensor_tensor(xT[j][:, 4 * b:4 * b + 4, :],
                                    bank[:, XT_BANKS[j][b], :].rearrange("p (k t) -> p k t", k=4),
                                    cols(gT[:, 4 * b:4 * b + 4], 4, P), ALU.mult).then_inc(xt_ready, 1)
            dve.wait_ge(sum_ready, 2)
            V.tensor_scalar(st[:, 2:4], st[:, 0:2], 1.0 / D, EPS, ALU.mult, ALU.add).then_inc(stat_v, 1)

            dve.wait_ge(setup_mm, 4)
            V.tensor_copy(gT[:, 8:36], bank[:, 7, 8:36]).then_inc(gT_ready, 1)
            dve.wait_ge(gT_ready, 2)
            for c in (24, 26):
                V.tensor_scalar(gT[:, c:c + 1], gT[:, c:c + 1], HD ** -0.5, None, ALU.mult).then_inc(gT_ready, 1)

            def head_sums(j, h0, h1, nth):
                dve.wait_ge(sq_ready, 3 * (j + 1))
                if j:
                    dve.wait_ge(stat_r, nth)
                ss = by_group(ss_h[:, :])[:, :, h0:h1]
                link(V.tensor_reduce(ss, sq[j].rearrange("p (g h d) -> p g h d", g=2, d=HD)[:, :, h0:h1, :], AX, ALU.add))
                V.tensor_scalar(ss, ss, 1.0 / HD, EPS, ALU.mult, ALU.add).then_inc(stat_v, 1)

            def k_sums(j):
                head_sums(j, 8, 10, 2)

            def q_sums(j):
                head_sums(j, 0, 8, 3)
                dve.sem_inc(ssh_ready, 1)

            pairs = qn.rearrange("p b (u d) -> p b u d", u=2)

            def heads_of(j, b, at, n):
                return bank[:, 3 * j + b, at:at + n * HD].rearrange("p (i d) -> p i d", d=HD)

            def raw_q(j):
                dve.wait_ge(sq_ready, 3 * j + 1)
                if j:
                    dve.wait_ge(qt_mm, 2)
                else:
                    dve.wait_ge(scr_out, 16)
                V.tensor_copy(pairs[:, 0:4].rearrange("p i u d -> p u i d"),
                              bank[:, 3 * j, :].rearrange("p (u i d) -> p u i d", u=2, d=HD)).then_inc(qn_ready, 1)
                dve.wait_ge(v_copied, 2 * j + 1)
                V.tensor_copy(pairs[:, 5:9, 0], heads_of(j, 1, 256, 4)).then_inc(qn_ready, 1)
                dve.wait_ge(v_copied, 2 * j + 2)
                V.tensor_copy(pairs[:, 5:9, 1], heads_of(j, 2, 0, 4)).then_inc(qn_ready, 1)

            def factors(j, h0, h1, nth):
                dve.wait_ge(stat_r, nth)
                f = by_group(f_h[:, j, :])[:, :, h0:h1]
                link(V.tensor_scalar(f, f, st[:, 2 + j:3 + j], None, ALU.mult))

            def normed_k(j):
                factors(j, 8, 10, 2 + 2 * j)
                if j:
                    dve.wait_ge(qt_mm, 3)
                V.tensor_tensor(pairs[:, 4], heads_of(j, 1, 0, 2), cols(f_h[:, j, 8:10], 2, HD),
                                ALU.mult).then_inc(qn_ready, 1)
                V.tensor_tensor(pairs[:, 9], heads_of(j, 2, 256, 2), cols(f_h[:, j, 20:22], 2, HD),
                                ALU.mult).then_inc(qn_ready, 1)

            def q_columns(j, b1, b2):
                dve.wait_ge(gT_ready, 4)
                dve.wait_ge(qt_mm, 3 * j + 2)
                V.tensor_scalar(qT[j][:, 1, :, :].rearrange("p i t -> p (i t)"), bank[:, b1, :],
                                gT[:, 26:27], None, ALU.mult).then_inc(qtb_ready, 1)
                dve.wait_ge(qt_mm, 3 * j + 3)
                for g in range(2):
                    V.tensor_scalar(kT[:, g, j * P:(j + 1) * P], bank[:, b2, g * P:(g + 1) * P],
                                    gT[:, 25 + 2 * g:26 + 2 * g], None, ALU.mult).then_inc(qtb_ready, 1)

            def softmax_max(j, c):
                n = 4 * j + c
                W = (j + 1) * P
                dve.wait_ge(s_mm, n + 1)
                if n >= 2:
                    dve.wait_ge(pt_mm, n - 1 if n <= 5 else 4 + 2 * (n - 5))
                dst = S_buf[:, n % 2, 0:4 * W].rearrange("p (i w) -> p i w", i=4)
                for i in range(4):
                    if j == 0:
                        src = bank[:, S0_BANKS[c], i * W:(i + 1) * W]
                    else:
                        src = bank[:, S1_BANKS[c][i // 2], (i % 2) * W:(i % 2 + 1) * W]
                    head = 12 * (c // 2) + 4 * (c % 2) + i
                    V.scalar_tensor_tensor(out=dst[:, i, :], in0=src, scalar=f_h[:, j, head:head + 1],
                                           in1=bias[:, 4 * c + i, W - 1::-1], op0=ALU.mult,
                                           op1=ALU.add).then_inc(dve_step, 1)
                chain[0] += 4
                dve.wait_ge(dve_step, chain[0])
                m = slice(4 * c, 4 * c + 4)
                link(V.tensor_reduce(mx[:, j, m], dst, AX, ALU.max))
                if c < 2:
                    link(V.tensor_tensor(mx[:, j, m], mx[:, j, m], sinks[:, m], ALU.max))
                V.tensor_scalar(negm[:, j, m], mx[:, j, m], -1.0, None, ALU.mult).then_inc(m_ready, 1)
                if c < 2:
                    dve.wait_ge(m_ready, n + 1)
                    V.tensor_tensor(snk[:, j, m], sinks[:, m], negm[:, j, m], ALU.add).then_inc(snk_ready, 1)

            def denominators(j, c):
                n = 4 * j + c
                m = slice(4 * c, 4 * c + 4)
                dve.wait_ge(exp_done, 4 * n + 4)
                if c < 2:
                    dve.wait_ge(snk_exp, 2 * j + c + 1)
                    link(V.tensor_tensor(rsum[:, j, m], rsum[:, j, m], snk_e[:, j, m], ALU.add))
                V.reciprocal(rden[:, j, m], rsum[:, j, m]).then_inc(den_ready, 1)

            def group_stats(j):
                dve.wait_ge(oss_mm, j + 1)
                V.tensor_scalar(st[:, 10 + 2 * j:12 + 2 * j], bank[:, 7, 0:2], 1.0 / 512, EPS,
                                ALU.mult, ALU.add).then_inc(stat_v, 1)

            def residual(j, g, n, nth):
                dve.wait_ge(stat_r, nth)
                dve.wait_ge(proj_mm, 4 * j + 2 * g + n + 1)
                if g:
                    dve.wait_ge(x1_ready, 4 * j + n + 1)
                xn = xs[:, j, n * 512:(n + 1) * 512]
                V.scalar_tensor_tensor(out=xn, in0=bank[:, PJ_BANKS[j][g][n], :], scalar=st[:, 10 + 2 * j + g:11 + 2 * j + g],
                                       in1=xn, op0=ALU.mult, op1=ALU.add).then_inc(x1_ready, 1)

            def x_stats(j):
                dve.wait_ge(sum_ready, 3 + j)
                V.tensor_scalar(st[:, 20 + j:21 + j], st[:, 34 + j:35 + j], 1.0 / D, EPS,
                                ALU.mult, ALU.add).then_inc(stat_v, 1)

            def router_gains():
                dve.wait_ge(route_in, 16 * 4)
                V.tensor_tensor(w_r[:, :, :], w_r[:, :, :], cols(gT[:, 28:36], KD, G + E),
                                ALU.mult).then_inc(wr_scaled, 1)

            raw_q(0)
            k_sums(0)
            q_sums(0)
            normed_k(0)
            q_columns(0, 7, 0)
            factors(0, 0, 8, 3)
            dve.wait_ge(bias_in, 16)
            dve.wait_ge(sinks_in, 16)
            softmax_max(0, 0)
            softmax_max(0, 1)
            denominators(0, 0)
            denominators(0, 1)
            softmax_max(0, 2)
            denominators(0, 2)
            softmax_max(0, 3)
            denominators(0, 3)
            raw_q(1)
            k_sums(1)
            q_sums(1)
            normed_k(1)
            q_columns(1, 6, 5)
            factors(1, 0, 8, 5)
            softmax_max(1, 0)
            router_gains()
            softmax_max(1, 1)
            group_stats(0)
            denominators(1, 0)
            denominators(1, 1)
            residual(0, 0, 0, 6)
            residual(0, 0, 1, 6)
            residual(0, 1, 0, 6)
            softmax_max(1, 2)
            denominators(1, 2)
            residual(0, 1, 1, 6)
            softmax_max(1, 3)
            denominators(1, 3)
            x_stats(0)

            keys = key.rearrange("p j r e -> p j (r e)")
            weights = weight[:, :, :, :].rearrange("p j r e -> p j (r e)")

            def select(i):
                V.tensor_tensor(
                    sel, iota[:, :].unsqueeze(1).unsqueeze(1).to_broadcast([P, NT, 2, SLOTS]),
                    keys[:, :, bass.ds(2 * i, 2)].unsqueeze(3).to_broadcast([P, NT, 2, SLOTS]),
                    ALU.is_equal).then_inc(sel_ready, 1)

            def weigh(i):
                dve.wait_ge(sel_ready, i + 1)
                V.tensor_tensor(
                    selw, sel,
                    weights[:, :, bass.ds(2 * i, 2)].unsqueeze(3).to_broadcast([P, NT, 2, SLOTS]),
                    ALU.mult).then_inc(selw_ready, 1)

            def choose(j, src, best, one_hot_out, n):
                link(V.scalar_tensor_tensor(out=rb[:, 0:n], in0=src, scalar=best, in1=first[:, 0:n],
                                            op0=ALU.is_equal, op1=ALU.mult))
                link(V.tensor_reduce(rs[:, j, 15:16], rb[:, 0:n], AX, ALU.max))
                link(V.tensor_scalar(one_hot_out, rb[:, 0:n], rs[:, j, 15:16], None, ALU.is_equal))

            def route(j):
                r = rs[:, j, :]
                L = lg_of(j)
                dve.wait_ge(consts, 3)
                dve.wait_ge(logit_mm, j + 1)
                dve.wait_ge(stat_r, 7 + 2 * j)
                link(V.scalar_tensor_tensor(out=L[:, :], in0=bank[:, 3 + j, 0:G + E], scalar=st[:, 20 + j:21 + j],
                                            in1=r_bias[:, :], op0=ALU.mult, op1=ALU.add))
                link(V.tensor_reduce(r[:, 0:1], L[:, 0:G], AX, ALU.max))
                V.tensor_scalar(r[:, 1:2], r[:, 0:1], -1.0, None, ALU.mult).then_inc(r_max, 1)
                choose(j, L[:, 0:G], r[:, 0:1], r[:, 11:11 + G], G)
                link(V.tensor_scalar(rb[:, 0:G], r[:, 11:11 + G], -1.0, -NEG, ALU.add, ALU.mult))
                link(V.tensor_tensor(em[:, :].rearrange("p (g e) -> p g e", g=G),
                                     L[:, G:].rearrange("p (g e) -> p g e", g=G),
                                     cols(rb[:, 0:G], G, EG), ALU.add))
                link(V.tensor_reduce(r[:, 2:3], em[:, :], AX, ALU.max))
                choose(j, em[:, :], r[:, 2:3], ra[:, 0, :], E)
                link(V.scalar_tensor_tensor(out=em[:, :], in0=ra[:, 0, :], scalar=2 * NEG, in1=em[:, :],
                                            op0=ALU.mult, op1=ALU.add))
                link(V.tensor_reduce(r[:, 3:4], em[:, :], AX, ALU.max))
                V.tensor_scalar(r[:, 10:11], r[:, 2:3], -1.0, None, ALU.mult).then_inc(r_max, 1)
                choose(j, em[:, :], r[:, 3:4], ra[:, 1, :], E)
                V.tensor_tensor(member[:, j, :], ra[:, 0, :], ra[:, 1, :], ALU.add).then_inc(member_ready, 1)

            def route_weights(j):
                r = rs[:, j, :]
                dve.wait_ge(r_exp, 2 * j + 2)
                link(V.tensor_scalar(r[:, 0:1], r[:, 9:10], 1.0, r[:, 8:9], ALU.add, ALU.mult))
                link(V.reciprocal(r[:, 1:2], r[:, 0:1]))
                link(V.tensor_tensor(r[:, 2:3], r[:, 1:2], r[:, 9:10], ALU.mult))
                link(V.tensor_scalar(rb[:, :], ra[:, 1, :], r[:, 2:3], None, ALU.mult))
                link(V.scalar_tensor_tensor(out=weight[:, j, 0, :], in0=ra[:, 0, :], scalar=r[:, 1:2], in1=rb[:, :],
                                            op0=ALU.mult, op1=ALU.add))

            route(0)
            route_weights(0)
            group_stats(1)
            for g in range(2):
                for n in range(2):
                    residual(1, g, n, 8)
            x_stats(1)
            route(1)
            dve.wait_ge(rank_mm, 1)
            ranks = bank[:, 7, 0:2 * E].rearrange("p (j e) -> p j e", j=NT)
            link(V.scalar_tensor_tensor(out=key[:, :, 0, :], in0=ranks, scalar=1.0, in1=member[:, :, :],
                                        op0=ALU.add, op1=ALU.mult))
            select(0)
            route_weights(1)
            dve.wait_ge(rank_mm, 2)
            link(V.tensor_reduce(counts[:, 0:1], bank[:, 4, 0:E], AX, ALU.max))
            for r in range(1, ROUNDS_MAX):
                link(V.tensor_scalar(counts[:, r:r + 1], counts[:, 0:1], float(SLOTS * r), None, ALU.is_gt))
            link(V.tensor_reduce(rs[:, 0, 0:1], counts[:, 1:ROUNDS_MAX], AX, ALU.add))
            for c, a, b in ((1, PAIRS, PAIRS), (2, 1, 1), (3, PAIRS, PAIRS - 2), (4, 1, 0)):
                link(V.tensor_scalar(rs[:, 0, c:c + 1], rs[:, 0, 0:1], float(a), float(b), ALU.mult, ALU.add))
            V.tensor_copy(n_i[:, :], rs[:, 0, 1:5]).then_inc(n_ready, 1)
            for r in range(1, ROUNDS_MAX):
                V.tensor_copy(weight[:, :, r, :], weight[:, :, 0, :]).then_inc(key_ready, 1)
                V.tensor_scalar(key[:, :, r, :], key[:, :, 0, :], -float(SLOTS * r), None,
                                ALU.add).then_inc(key_ready, 1)
            dve.wait_ge(key_ready, 2 * (ROUNDS_MAX - 1))

            def add_mix(i, j):
                for n in range(2):
                    dve.wait_ge(mix_mm, 4 * i + (2 * j + n + 1))
                    xn = xs[:, j, n * 512:(n + 1) * 512]
                    V.tensor_tensor(xn, xn, bank[:, 4 * j + n, :], ALU.add).then_inc(mix_added, 1)

            def pair_step(previous, has_next):
                i = 0 if previous is None else previous + 1
                if previous is not None:
                    dve.wait_ge(swt_mm, previous + 1)
                weigh(i)
                if has_next:
                    dve.wait_ge(gather_mm, 2 * i + 2)
                    dve.wait_ge(selw_ready, i + 1)
                    select(i + 1)
                if previous is not None:
                    add_mix(previous, 0)
                dve.wait_ge(silu_ready, i + 1)
                dve.wait_ge(slots_read, RING * i + 8)
                V.tensor_tensor(act, silu, bank[:, 3, :], ALU.mult).then_inc(act_ready, 1)
                if previous is not None:
                    add_mix(previous, 1)
                dve.wait_ge(slots_read, RING * i + 12)
                V.tensor_copy(y_sb[:, 512:1024], bank[:, 7, :]).then_inc(y1_ready, 1)

            pair_step(None, True)
            dve.wait_ge(pp_out, 7)
            a = st[:, 40:44].rearrange("p (j n) -> p j n", j=NT)
            link(V.tensor_tensor(st[:, 44:46], a[:, :, 0], a[:, :, 1], ALU.add))
            V.tensor_scalar(st[:, 44:46], st[:, 44:46], 1.0 / D, EPS, ALU.mult, ALU.add).then_inc(pp_var, 1)
            dve.wait_ge(pp_var, 1)
            dve.wait_ge(pp_root, 1)
            link(V.reciprocal(st[:, 54:56], st[:, 46:48]))
            link(V.tensor_tensor(st[:, 56:58], st[:, 54:56], st[:, 54:56], ALU.mult))
            link(V.tensor_tensor(st[:, 56:58], st[:, 56:58], st[:, 44:46], ALU.mult))
            link(V.tensor_scalar(st[:, 56:58], st[:, 56:58], -0.5, 1.5, ALU.mult, ALU.add))
            link(V.tensor_tensor(st[:, 54:56], st[:, 54:56], st[:, 56:58], ALU.mult))
            for j in range(NT):
                V.scalar_tensor_tensor(out=PL[:, j, :], in0=PL[:, j, :], scalar=st[:, 54 + j:55 + j],
                                       in1=gB[:, :], op0=ALU.mult, op1=ALU.mult).then_inc(mix_added, 2)

            dve.wait_ge(n_ready, 1)
            before_last = dve.value_load(n_i[0:1, 2:3], min_val=PAIRS - 2, max_val=PAIRS * ROUNDS_MAX - 2)
            with dve.Fori(0, before_last) as previous:
                pair_step(previous, True)
            pair_step(before_last, False)
            add_mix(before_last + 1, 0)
            add_mix(before_last + 1, 1)

            for j in range(NT):
                dve.wait_ge(xf_mm, 2 * j + 2)
                V.tensor_copy(xfT[:, j, 4:8, :].rearrange("p k t -> p (k t)"),
                              bank[:, 3 - 2 * j, :]).then_inc(xfb_ready, 1)
                dve.wait_ge(sum_ready, 5 + j)
                V.tensor_scalar(st[:, 50 + j:51 + j], st[:, 48 + j:49 + j], 1.0 / D, EPS,
                                ALU.mult, ALU.add).then_inc(stat_v, 1)
            for n, (j, c0, width, b) in enumerate(GATE):
                c = slice(c0, c0 + width)
                dve.wait_ge(gate_ready, n + 1)
                link(V.tensor_tensor(result[:, j, c], gate[:, j, c], PL[:, j, c], ALU.mult))
                V.tensor_tensor(result[:, j, c], result[:, j, c], xs[:, j, c], ALU.add).then_inc(res_ready, 1)


INPUTS = ["x", "p", "rel_bias", "attn_norm", "w_in", "swa_q_norm", "swa_k_norm", "swa_sinks",
          "moba_q_norm", "moba_k_norm", "swa_out_norm", "moba_out_norm", "w_out", "ffn_norm",
          "w_router_group", "b_router_group", "w_router_expert", "b_router_expert",
          "w_exp_gate", "w_exp_up", "w_exp_down", "ple_norm", "w_ple_gate", "w_ple_proj", "ple_out_norm"]


def kernel(**inputs):
    import concourse.bacc as bacc
    from concourse.bass_utils import run_bass_kernel_spmd

    nc = bacc.Bacc("TRN2", target_bir_lowering=False, num_devices=1)
    arrays, t = {}, {}
    given = {name: np.ascontiguousarray(inputs[name]) for name in INPUTS}
    given["bucket_one_hot"] = bucket_one_hot()
    for name, a in given.items():
        arrays[f"in_{name}"] = a
        t[name] = nc.dram_tensor(f"in_{name}", a.shape, mybir.dt.from_np(a.dtype), kind="ExternalInput").ap()
    out = nc.dram_tensor("out", inputs["x"].shape, F32, kind="ExternalOutput").ap()
    build_program(nc, t, out)
    r = run_bass_kernel_spmd(nc, [arrays], core_ids=[0])
    return r.results[0]["out"]
```
